# Optimizing a Trainium2 kernel written in Bass

```python
import jax, jax.numpy as jnp
from jax import lax
import numpy as np

D_MODEL = 1024
BATCH = 1
SEQ = 512
DEPTH = 2

N_META = 16
BLOCK = 128
WINDOW = 128
ROPE_THETA = 10000.0
EPS = 1e-6
NEG = -1e30
SWA_HEADS = 8
SWA_KV_HEADS = 2
SWA_HEAD_DIM = 64
SWA_GROUP = SWA_HEADS // SWA_KV_HEADS
MLA_HEADS = 8
MLA_Q_RANK = 256
MLA_KV_RANK = 128
MLA_NOPE_DIM = 64
MLA_ROPE_DIM = 32
MLA_V_DIM = 64
MLA_QK_DIM = MLA_NOPE_DIM + MLA_ROPE_DIM
SWA_Q_W = SWA_HEADS * SWA_HEAD_DIM
SWA_KV_W = SWA_KV_HEADS * SWA_HEAD_DIM
MLA_OUT_W = MLA_HEADS * MLA_V_DIM
MIX_W = SWA_Q_W + MLA_OUT_W
IN_W = SWA_Q_W + 2 * SWA_KV_W + MLA_Q_RANK + MLA_KV_RANK + MLA_ROPE_DIM
D_FF = -(-8 * D_MODEL // (3 * 256)) * 256

kernel_name = "hymba_swa_sink_mla_hybrid"

def rmsnorm(x, g):
    xf = x.astype(jnp.float32)
    y = xf * lax.rsqrt(jnp.mean(xf * xf, axis=-1, keepdims=True) + EPS)
    return (y * g.astype(jnp.float32)).astype(x.dtype)

def rope(x, pos):
    d = x.shape[-1]
    inv = ROPE_THETA ** (-jnp.arange(0, d, 2, dtype=jnp.float32) / d)
    ang = pos[:, None] * inv[None, :]
    cos = jnp.cos(ang)[:, None, :]
    sin = jnp.sin(ang)[:, None, :]
    xf = x.astype(jnp.float32)
    x1, x2 = xf[..., : d // 2], xf[..., d // 2:]
    return jnp.concatenate([x1 * cos - x2 * sin, x2 * cos + x1 * sin], -1).astype(x.dtype)

def swa_sink_attention(q, k, v, sinks, key_valid):
    B, T, _, D = q.shape
    nb = T // BLOCK
    qb = q.reshape(B, nb, BLOCK, SWA_KV_HEADS, SWA_GROUP, D)
    kb = k.reshape(B, nb, BLOCK, SWA_KV_HEADS, D)
    vb = v.reshape(B, nb, BLOCK, SWA_KV_HEADS, D)
    prev = lambda a: jnp.concatenate([jnp.zeros_like(a[:, :1]), a[:, :-1]], axis=1)
    kw = jnp.concatenate([prev(kb), kb], axis=2)
    vw = jnp.concatenate([prev(vb), vb], axis=2)
    s = jnp.einsum("bnqhgd,bnkhd->bhgnqk", qb, kw,
                   preferred_element_type=jnp.float32) * (D ** -0.5)
    qpos = jnp.arange(T).reshape(nb, BLOCK)
    kpos = jnp.concatenate([qpos - BLOCK, qpos], axis=1)
    kv_ok = key_valid.reshape(nb, BLOCK)
    kv_ok = jnp.concatenate(
        [jnp.concatenate([jnp.zeros((1, BLOCK), bool), kv_ok[:-1]], 0), kv_ok], 1)
    diff = qpos[:, :, None] - kpos[:, None, :]
    mask = (diff >= 0) & (diff < WINDOW) & kv_ok[:, None, :]
    s = jnp.where(mask, s, NEG)
    sink = jnp.broadcast_to(
        sinks.astype(jnp.float32).reshape(SWA_KV_HEADS, SWA_GROUP)[None, :, :, None, None, None],
        s.shape[:-1] + (1,))
    p = jax.nn.softmax(jnp.concatenate([s, sink], axis=-1), axis=-1)[..., :-1]
    o = jnp.einsum("bhgnqk,bnkhd->bnqhgd", p.astype(v.dtype), vw)
    return o.reshape(B, T, SWA_HEADS * D)

def causal_block_attention(q, k, v, key_valid):
    B, T, H, dqk = q.shape
    nb = T // BLOCK
    scale = dqk ** -0.5
    qb = jnp.moveaxis(q.reshape(B, nb, BLOCK, H, dqk), 1, 0)
    kpos = jnp.arange(T)

    def one_block(args):
        qblk, i = args
        s = jnp.einsum("bqhd,bkhd->bhqk", qblk, k,
                       preferred_element_type=jnp.float32) * scale
        qpos = i * BLOCK + jnp.arange(BLOCK)
        mask = (kpos[None, :] <= qpos[:, None]) & key_valid[None, :]
        p = jax.nn.softmax(jnp.where(mask, s, NEG), axis=-1)
        return jnp.einsum("bhqk,bkhd->bqhd", p.astype(v.dtype), v)

    o = lax.map(one_block, (qb, jnp.arange(nb)))
    return jnp.moveaxis(o, 0, 1).reshape(B, T, H * v.shape[-1])

def setup_inputs(seed: int = 0) -> dict:
    key = jax.random.key(seed)
    ks = jax.random.split(key, 20)
    f32 = jnp.float32
    nrm = lambda k, shape, scale: jax.random.normal(k, shape, f32) * scale
    gain = lambda k, shape: 1.0 + 0.02 * jax.random.normal(k, shape, f32)
    return {
        "x": nrm(ks[0], (BATCH, SEQ, D_MODEL), 1.0),
        "meta_tokens": nrm(ks[1], (N_META, D_MODEL), 1.0),
        "attn_norm": gain(ks[2], (DEPTH, D_MODEL)),
        "w_in": nrm(ks[3], (DEPTH, D_MODEL, IN_W), D_MODEL ** -0.5),
        "q_norm": gain(ks[4], (DEPTH, MLA_Q_RANK)),
        "w_q_up": nrm(ks[5], (DEPTH, MLA_Q_RANK, MLA_HEADS * MLA_QK_DIM), MLA_Q_RANK ** -0.5),
        "kv_norm": gain(ks[6], (DEPTH, MLA_KV_RANK)),
        "w_kv_up": nrm(ks[7], (DEPTH, MLA_KV_RANK, MLA_HEADS * (MLA_NOPE_DIM + MLA_V_DIM)),
                        MLA_KV_RANK ** -0.5),
        "sinks": nrm(ks[8], (DEPTH, SWA_HEADS), 1.0),
        "out_norm_swa": gain(ks[9], (DEPTH, SWA_Q_W)),
        "out_norm_mla": gain(ks[10], (DEPTH, MLA_OUT_W)),
        "w_o": nrm(ks[11], (DEPTH, MIX_W, D_MODEL), MIX_W ** -0.5),
        "ffn_norm": gain(ks[12], (DEPTH, D_MODEL)),
        "w_gate": nrm(ks[13], (DEPTH, D_MODEL, D_FF), D_MODEL ** -0.5),
        "w_up": nrm(ks[14], (DEPTH, D_MODEL, D_FF), D_MODEL ** -0.5),
        "w_down": nrm(ks[15], (DEPTH, D_FF, D_MODEL), D_FF ** -0.5),
        "final_norm": gain(ks[16], (D_MODEL,)),
    }

def reference(x, meta_tokens, attn_norm, w_in, q_norm, w_q_up, kv_norm, w_kv_up, sinks,
              out_norm_swa, out_norm_mla, w_o, ffn_norm, w_gate, w_up, w_down, final_norm):
    B, S, D = x.shape
    front = (-N_META) % BLOCK
    back = (-S) % BLOCK
    T = front + N_META + S + back
    h = jnp.concatenate([
        jnp.zeros((B, front, D), x.dtype),
        jnp.broadcast_to(meta_tokens.astype(x.dtype)[None], (B, N_META, D)),
        x,
        jnp.zeros((B, back, D), x.dtype)], axis=1)
    idx = jnp.arange(T)
    key_valid = (idx >= front) & (idx < front + N_META + S)
    pos = (idx - front).astype(jnp.float32)

    o1 = SWA_Q_W
    o2 = o1 + SWA_KV_W
    o3 = o2 + SWA_KV_W
    o4 = o3 + MLA_Q_RANK
    o5 = o4 + MLA_KV_RANK
    for l in range(DEPTH):
        u = rmsnorm(h, attn_norm[l])
        proj = u @ w_in[l]
        q_a = rope(proj[..., :o1].reshape(B, T, SWA_HEADS, SWA_HEAD_DIM), pos)
        k_a = rope(proj[..., o1:o2].reshape(B, T, SWA_KV_HEADS, SWA_HEAD_DIM), pos)
        v_a = proj[..., o2:o3].reshape(B, T, SWA_KV_HEADS, SWA_HEAD_DIM)
        out_a = swa_sink_attention(q_a, k_a, v_a, sinks[l], key_valid)
        q_b = (rmsnorm(proj[..., o3:o4], q_norm[l]) @ w_q_up[l]).reshape(
            B, T, MLA_HEADS, MLA_QK_DIM)
        kv_b = (rmsnorm(proj[..., o4:o5], kv_norm[l]) @ w_kv_up[l]).reshape(
            B, T, MLA_HEADS, MLA_NOPE_DIM + MLA_V_DIM)
        k_rope = rope(proj[..., o5:][:, :, None, :], pos)
        q_full = jnp.concatenate(
            [q_b[..., :MLA_NOPE_DIM], rope(q_b[..., MLA_NOPE_DIM:], pos)], axis=-1)
        k_full = jnp.concatenate(
            [kv_b[..., :MLA_NOPE_DIM],
             jnp.broadcast_to(k_rope, (B, T, MLA_HEADS, MLA_ROPE_DIM))], axis=-1)
        v_b = kv_b[..., MLA_NOPE_DIM:]
        out_b = causal_block_attention(q_full, k_full, v_b, key_valid)
        mix = jnp.concatenate([rmsnorm(out_a, out_norm_swa[l]),
                               rmsnorm(out_b, out_norm_mla[l])], axis=-1)
        h = h + mix @ w_o[l]
        u = rmsnorm(h, ffn_norm[l])
        h = h + (jax.nn.silu(u @ w_gate[l]) * (u @ w_up[l])) @ w_down[l]

    h = rmsnorm(h, final_norm)
    start = front + N_META
    return h[:, start:start + S]


_drawn_inputs = setup_inputs


def setup_inputs(seed=0):
    import zlib

    import numpy as np

    out = dict(_drawn_inputs(seed))
    spreads = {}
    factors = {'q_norm': 5.653,
     'kv_norm': 2.779,
     'sinks': 3.827,
     'out_norm_swa': 3.731,
     'out_norm_mla': 3.743,
     'ffn_norm': 4.056,
     'final_norm': 2.84}
    for name, (base, spread) in spreads.items():
        noise = np.random.default_rng([zlib.crc32(name.encode()), seed]).standard_normal(out[name].shape)
        drawn = base * np.exp(spread * noise) if base else spread * noise
        out[name] = __import__('jax').numpy.asarray(drawn.astype(out[name].dtype))
    for name, factor in factors.items():
        out[name] = (out[name] * factor).astype(out[name].dtype)
    return out
```

```python
from contextlib import ExitStack

import numpy as np

import concourse.bass as bass
from concourse import mybir

F32 = mybir.dt.float32
F32R = mybir.dt.float32r
ALU = mybir.AluOpType
ACT = mybir.ActivationFunctionType
AX = mybir.AxisListType

P = 128
D_MODEL = 1024
DEPTH = 2
N_META = 16
SEQ = 512
T = N_META + SEQ
NB = SEQ // P
EPS = 1e-6
NEG = -1e30
HEADS = 8
SWA_DIM = 64
Q_RANK = 256
KV_RANK = 128
NOPE = 64
ROPE = 32
V_DIM = 64
SWA_SCALE = SWA_DIM ** -0.5
MLA_SCALE = (NOPE + ROPE) ** -0.5
D_FF = -(-8 * D_MODEL // (3 * 256)) * 256
KT = D_MODEL // P
FT = D_FF // P
UNIT = KT * P
CHUNK = T // 2

U_IN, U_KV, U_Q, U_O, U_GU, U_DOWN = 0, 10, 11, 13, 21, 21 + 2 * FT
DOWN_PARTS = (6, 6, 5, 5)
DOWN_AT = (0, 6, 12, 17)
UNITS = U_DOWN + KT * len(DOWN_PARTS)
RAW, SPLIT = 4, 2

PROJ = ["kva", "S1", "kr", "qa0", "qa1", "Skv", "KRS", "ka", "va", "Sq", "q0", "q1", "q2", "q3", "VA",
        "n0", "n1", "n2", "n3", "v0", "v1", "VT0", "v2", "VT1", "v3", "VT2", "H0", "VT3",
        "H1", "H2", "H3", "H4", "H5", "H6", "H7"]
DRAIN = ["S1", "kva"] + PROJ[2:]
UNIT_OF = {"kva": 0, "kr": 1, "qa0": 2, "qa1": 3, "ka": 4, "va": 5, "q0": 6, "q1": 7, "q2": 8, "q3": 9}
A_G = len(PROJ)
A_O = A_G + 2
A_F = A_O + KT
A_D = A_F + 2 * FT + 1
ACCS = A_D + KT
STAT_TILES = [KT, 1, 2, 4, 4, KT]
ST_ATTN, ST_KV, ST_Q, ST_SWA, ST_MLA, ST_FFN = range(6)
STATS = len(STAT_TILES)

C_ID, C_ONES, C_SEL, C_MASK, C_COS, C_SIN, C_TBL = 0, 128, 256, 320, 576, 576 + T, 576 + 2 * T
C_END = 576 + 3 * T
G_ATTN, G_FFN, G_Q, G_KV, G_SWA, G_MLA, G_SINK, G_LAYER = 0, 8, 16, 18, 19, 23, 27, 35
G_FINAL = DEPTH * G_LAYER


def build(nc, xT, consts, gains, w_in, w_kv, w_q, w_o, w_gate, w_up, w_down, out):
    ctx = ExitStack()
    with ctx:
        base = nc.sbuf_base
        at = [-(-base // 64) * 64]

        def place(name, shape, dt=F32, offset=None):
            size = 4 * int(np.prod(shape[1:]))
            if offset is None:
                offset = at[0]
                at[0] += -(-size // 32) * 32
            return nc.alloc_sbuf_tensor_at(name, shape, dt, offset=offset)

        def sem(name):
            return ctx.enter_context(nc.semaphore(name))

        h = place("h", [P, KT, T])
        u_hi = place("u_hi", [P, KT, T], F32R)
        u_lo = place("u_lo", [P, KT, T], F32R)
        raw = place("raw", [P, RAW, UNIT])
        w_hi = place("w_hi", [P, SPLIT, UNIT], F32R)
        w_lo = place("w_lo", [P, SPLIT, UNIT], F32R)
        x0 = at[0]
        act_hi = place("act_hi", [P, FT, T], F32R)
        act_lo = place("act_lo", [P, FT, T], F32R)
        x1 = at[0]
        at[0] = x0
        q_swa = place("q_swa", [P, 4, T])
        k_swa = place("k_swa", [P, T])
        v_swa = place("v_swa", [P, NB, P])
        v_swa_meta = place("v_swa_meta", [N_META, P])
        mix_at = at[0]
        q_mla = place("q_mla", [P, HEADS, T])
        k_mla = place("k_mla", [P, HEADS, T])
        mix_hi = place("mix_hi", [P, KT, T], F32R, offset=mix_at)
        mix_lo = place("mix_lo", [P, KT, T], F32R, offset=mix_at + 4 * KT * T)
        v_mla = place("v_mla", [P, NB, HEADS * V_DIM])
        v_mla_meta = place("v_mla_meta", [N_META, HEADS * V_DIM])
        soft_at = at[0]
        p_cols = 400 + P + 1
        probs = place("probs", [P, 3, p_cols])
        pT = place("pT", [P, 2, NB * P])
        pT_meta = place("pT_meta", [N_META, 2, P])
        vT_mla = place("vT_mla", [P, 4, T], offset=soft_at)
        vT_swa = place("vT_swa", [P, T], offset=soft_at + 4 * 4 * T)
        o_at = at[0]
        oT = place("oT", [P, 8, T])
        c_hi = place("c_hi", [P, 3, T], F32R, offset=o_at)
        c_lo = place("c_lo", [P, 3, T], F32R, offset=o_at + 4 * 3 * T)
        sin_r = place("sin_r", [P, T], offset=o_at + 4 * 6 * T)
        cos_r = place("cos_r", [P, T], offset=o_at + 4 * 7 * T)
        r_kv = place("r_kv", [P, T])
        assert at[0] <= x1, (at[0], x1)
        at[0] = max(at[0], x1)
        cst = place("cst", [P, C_END])
        gn = place("gn", [P, G_FINAL + KT])
        ident_r = place("ident_r", [P, P], F32R)
        mask_r = place("mask_r", [P, 2 * P], F32R)
        r_main = place("r_main", [P, T])
        r_q = place("r_q", [P, T])
        tbl_r = place("tbl_r", [P, T])
        var = place("var", [P, T])
        sq = place("sq", [P, T])
        sq_sum = place("sq_sum", [P, T])
        z = at[0]
        c_raw = place("c_raw", [P, 3, T])
        swapped = place("swapped", [P, T])
        rot_a = place("rot_a", [P, T])
        rot_b = place("rot_b", [P, T])
        gate = place("gate", [P, 2, T], offset=z)
        up = place("up", [P, 2, T], offset=z + 8 * T)
        neg_max = place("neg_max", [P, 3])
        row_sum = place("row_sum", [P, 3])
        inv_sum = place("inv_sum", [P, 3])
        ms = place("ms", [N_META, HEADS, N_META + 1], offset=z)
        mrow = place("mrow", [N_META, 3, HEADS], offset=z + 640)
        mpT = place("mpT", [N_META, HEADS * N_META], offset=z + 768)
        assert at[0] <= nc.sbuf_usable_end, (at[0], nc.sbuf_usable_end)
        kr_t, kr_sum = rot_a, rot_b
        final = place("final", [P, KT, SEQ], offset=x0)

        ident = cst[:, C_ID:C_ID + P]
        ones = cst[:, C_ONES:C_ONES + P]
        sel = cst[0:64, C_SEL:C_SEL + 64]
        cos_t = cst[:, C_COS:C_COS + T]
        sin_t = cst[:, C_SIN:C_SIN + T]
        tbl = cst[:, C_TBL:C_TBL + T]

        ps = ctx.enter_context(nc.psum_tensor("ps", [P, 8, 512], F32))

        consts_landed = sem("consts_landed")
        h_landed = [sem(f"h_landed{k}") for k in range(KT)]
        raw_landed = [sem(f"raw_landed{k}") for k in range(RAW)]
        hi_ready = sem("hi_ready")
        lo_ready = sem("lo_ready")
        unit_used = sem("unit_used")
        acc_ready = sem("acc_ready")
        drained = sem("drained")
        masks_ready = sem("masks_ready")
        uh_ready = sem("uh_ready")
        u_ready = sem("u_ready")
        sq_made = sem("sq_made")
        sq_added = sem("sq_added")
        var_ready = sem("var_ready")
        r_ready = sem("r_ready")
        tables_ready = sem("tables_ready")
        ch_ready = sem("ch_ready")
        c_ready = sem("c_ready")
        swap_ready = sem("swap_ready")
        rot_step = sem("rot_step")
        krope_ready = sem("krope_ready")
        s_ready = sem("s_ready")
        max_ready = sem("max_ready")
        exp_ready = sem("exp_ready")
        inv_ready = sem("inv_ready")
        p_ready = sem("p_ready")
        pT_done = sem("pT_done")
        pT_copied = sem("pT_copied")
        pTm_copied = sem("pTm_copied")
        pv_done = sem("pv_done")
        o_copied = sem("o_copied")
        m_pe = sem("m_pe")
        m_dve = sem("m_dve")
        m_exp = sem("m_exp")
        mixf_ready = sem("mixf_ready")
        mixh_ready = sem("mixh_ready")
        mix_ready = sem("mix_ready")
        silu_done = sem("silu_done")
        prod_ready = sem("prod_ready")
        acth_ready = sem("acth_ready")
        act_ready = sem("act_ready")
        final_ready = sem("final_ready")
        stored = sem("stored")

        def unit0(L):
            return L * UNITS

        def acc0(L):
            return L * ACCS

        def stat(L, k):
            return L * STATS + k

        def made0(L, k):
            return L * sum(STAT_TILES) + sum(STAT_TILES[:k])

        def added0(L, k):
            return made0(L, k) + stat(L, k)

        def stat_acc(L, k):
            names = {ST_ATTN: "S1", ST_KV: "Skv", ST_Q: "Sq"}
            if L == DEPTH:
                return acc0(DEPTH)
            return acc0(L) + (PROJ.index(names[k]) if k in names else A_G + k - ST_SWA if k < ST_FFN else A_F + 1)

        def wait_sum_read(eng, L, k):
            if stat(L, k):
                eng.wait_ge(acc_ready, (stat_acc(L, k - 1) if k else stat_acc(L - 1, STATS - 1)) + 1)

        def wait_used(eng, n, it=0):
            L, r = divmod(n, UNITS)
            if r >= U_DOWN:
                m, x = divmod(r - U_DOWN, 4)
                if x < 3:
                    eng.wait_ge(unit_used, it * 3 + (3 * (KT * L + m) + x + 1))
                else:
                    eng.wait_ge(acc_ready, it + (acc0(L) + A_D + m + 1))
                return
            if r >= U_GU:
                j = r - U_GU
                a = A_F + (j + 1 if j else 0)
            elif r >= U_O:
                a = A_O + r - U_O
            else:
                a = PROJ.index({U_KV: "v3", U_Q: "H3", U_Q + 1: "H7"}.get(r) or
                               next(k for k, u in UNIT_OF.items() if u == r))
            eng.wait_ge(acc_ready, it * 4 + (acc0(L) + a + 1))

        def first(L):
            return 0 if L < DEPTH - 1 else N_META

        def chunks(L):
            return [(0, CHUNK), (CHUNK, CHUNK)] if L < DEPTH - 1 else [(N_META, SEQ)]

        def acc_view(slot, L, lo=0, hi=P):
            if L < DEPTH - 1:
                return ps[lo:hi, 2 * slot:2 * slot + 2, 0:CHUNK]
            return ps[lo:hi, 2 * slot, 0:SEQ]

        def tok_view(tile, L):
            if L < DEPTH - 1:
                return tile.rearrange("p (c n) -> p c n", c=2)
            return tile[:, N_META:T]

        def f32(ap):
            return ap.bitcast(F32)

        def drain_rank(name):
            return DRAIN.index(name) + 1

        def attn_blocks():
            for g in range(2):
                for p in range(4):
                    for half in range(2):
                        head = p + 4 * half if g == 0 else 2 * p + half
                        for b in range(NB):
                            yield g, head, b, p, half

        BLOCKS = list(attn_blocks())
        GB = len(BLOCKS) // 2

        def key_range(g, b):
            diag = N_META + P * b
            if g == 0 and b:
                return diag - P, P, [b - 1], False
            return 0, diag, list(range(b)), True

        def mix_part(dve, L, t, f):
            dve.wait_ge(mixh_ready, L * KT + t + 1)
            dve.tensor_tensor(mix_lo[:, t, f:], oT[:, t, f:], f32(mix_hi[:, t, f:]), ALU.subtract)\
               .then_inc(mix_ready, 1)

        def ffn_u(dve, u_part, L, m, f):
            g = L * G_LAYER + G_FFN + m
            dve.wait_ge(drained, acc0(L) + A_O + m + 1)
            u_part(m, gn[:, g:g + 1], f, 2 * KT * L + KT + m)

        block = ctx.enter_context(nc.Block())

        @block.sync
        def _(sp):
            def load(n, src, width=UNIT, it=0):
                slot = n % RAW
                if n >= RAW:
                    sp.wait_ge(lo_ready, it * 4 + (n - RAW + 1))
                sp.dma_start(raw[:, slot, 0:width], src).then_inc(raw_landed[slot], 16)

            for k in range(KT):
                if k == 0:
                    sp.dma_start(gn[:, :], gains).then_inc(consts_landed, 16)
                sp.dma_start(h[:, k, :], xT[k]).then_inc(h_landed[k], 16)
                if k in (1, 4):
                    n = 0 if k == 1 else 1
                    load(n, w_in[0, n])
            sp.dma_start(cst[:, :], consts).then_inc(consts_landed, 16)
            for L in range(DEPTH):
                n0 = unit0(L)
                for j in range(2 if L == 0 else 0, 10):
                    load(n0 + j, w_in[L, j])
                load(n0 + U_KV, w_kv[L])
                for j in range(2):
                    load(n0 + U_Q + j, w_q[L, j])
                for j in range(KT):
                    load(n0 + U_O + j, w_o[L, j])
                with sp.Fori(0, FT // 2) as i:
                    for c in range(4):
                        w = w_gate if c % 2 == 0 else w_up
                        load(n0 + U_GU + c, w[L, i * 2 + c // 2], it=i)
                with sp.Fori(0, KT) as i:
                    for c, (k0, kn) in enumerate(zip(DOWN_AT, DOWN_PARTS)):
                        load(n0 + U_DOWN + c, w_down[L, i, :, k0 * P:(k0 + kn) * P], kn * P, it=i)
            for m in range(KT):
                sp.wait_ge(final_ready, m + 1)
                sp.dma_start(out[m], final[:, m, :]).then_inc(stored, 16)
            sp.wait_ge(stored, 16 * KT)

        @block.gpsimd
        def _(pool):
            def sums(L, k):
                f = 0 if k < ST_SWA else first(L)
                a0 = added0(L, k)
                wait_sum_read(pool, L, k)
                pool.memset(sq_sum[:, :], 0.0).then_inc(sq_added, 1)
                for j in range(STAT_TILES[k]):
                    pool.wait_ge(sq_made, made0(L, k) + j + 1)
                    pool.wait_ge(sq_added, a0 + j + 1)
                    pool.tensor_tensor(sq_sum[:, f:], sq_sum[:, f:], sq[:, f:], ALU.add).then_inc(sq_added, 1)

            def product(f, L, par, step=0):
                pool.wait_ge(silu_done, step + (L * FT + f + 1))
                pool.wait_ge(drained, step * 2 + (acc0(L) + A_F + 2 * f + 3))
                t = first(L)
                pool.tensor_tensor(up[:, par, t:], gate[:, par, t:], up[:, par, t:], ALU.mult)\
                    .then_inc(prod_ready, 1)

            sums(0, ST_ATTN)
            for L in range(DEPTH):
                for k in (ST_KV, ST_Q, ST_SWA, ST_MLA, ST_FFN):
                    sums(L, k)
                with pool.Fori(0, FT // 2) as i:
                    for c in range(2):
                        product(c, L, c, step=i * 2)
                f = first(L)
                a0, m0 = added0(L + 1, 0), made0(L + 1, 0)
                wait_sum_read(pool, L + 1, 0)
                pool.memset(sq_sum[:, :], 0.0).then_inc(sq_added, 1)
                with pool.Fori(0, KT) as i:
                    pool.wait_ge(sq_made, i + m0 + 1)
                    pool.wait_ge(sq_added, i + a0 + 1)
                    pool.tensor_tensor(sq_sum[:, f:], sq_sum[:, f:], sq[:, f:], ALU.add).then_inc(sq_added, 1)

        @block.scalar
        def _(act):
            def hi(n, width=UNIT, it=0):
                act.wait_ge(raw_landed[n % RAW], it * 16 + 16 * (n // RAW + 1))
                if n >= SPLIT:
                    wait_used(act, n - SPLIT, it)
                act.activation(w_hi[:, n % SPLIT, 0:width], raw[:, n % RAW, 0:width], ACT.Copy)\
                   .then_inc(hi_ready, 1)

            def square(src, L, k, j, f=0, step=0):
                act.wait_ge(sq_added, step + (added0(L, k) + j + 1))
                if not isinstance(step, int):
                    act.nop(nofuse=True)
                act.activation(sq[:, f:], src, ACT.Square).then_inc(sq_made, 1)

            def gained(m, gain, f):
                act.activation(u_hi[:, m, f:], h[:, m, f:], ACT.Copy, scale=gain).then_inc(uh_ready, 1)

            def root(L, k, dst, f=0):
                act.wait_ge(var_ready, stat(L, k) + 1)
                act.activation(dst[:, f:], var[:, f:], ACT.Sqrt).then_inc(r_ready, 1)

            def latent(L, j, k, jj):
                act.wait_ge(drained, acc0(L) + drain_rank(["kva", "qa0", "qa1"][j]))
                g = gn[:, L * G_LAYER + (G_KV if j == 0 else G_Q + j - 1):][:, 0:1]
                act.activation(c_hi[:, j, :], c_raw[:, j, :], ACT.Copy, scale=g).then_inc(ch_ready, 1)
                square(c_raw[:, j, :], L, k, jj)

            def swap(L, name, scale, before):
                a = PROJ.index(name)
                s = a % 4
                act.wait_ge(acc_ready, acc0(L) + a + 1)
                if before:
                    act.wait_ge(drained, acc0(L) + drain_rank(before))
                for qd in range(4):
                    o = 32 * (qd ^ 1)
                    ins = act.activation(swapped[o:o + 32, :].rearrange("p (c n) -> p c n", c=2),
                                         ps[32 * qd:32 * qd + 32, 2 * s:2 * s + 2, 0:CHUNK],
                                         ACT.Copy, scale=scale)
                ins.then_inc(swap_ready, 1)

            def attention(L, g):
                def copy_pT(i):
                    _, _, b, _, _ = BLOCKS[g * GB + i]
                    U = L * 2 * GB + g * GB + i
                    width = P * (1 + len(key_range(g, b)[2]))
                    act.wait_ge(pT_done, U + 1)
                    if U >= 2:
                        act.wait_ge(pv_done, U - 1)
                    act.activation(pT[:, U % 2, 0:width], ps[:, 2 * (U % 3), 0:width], ACT.Copy)\
                       .then_inc(pT_copied, 1)

                for i in range(GB + 3):
                    if i >= 3:
                        copy_pT(i - 3)
                    if i < GB:
                        _, _, b, _, _ = BLOCKS[g * GB + i]
                        U = L * 2 * GB + g * GB + i
                        n_off = key_range(g, b)[1]
                        extra = 1 if g == 0 else 0
                        s = 2 * (U % 3)
                        act.wait_ge(max_ready, U + 1)
                        if U >= 3:
                            act.wait_ge(pT_done, U - 2)
                        act.activation(probs[:, U % 3, 400 - n_off:400 + P + extra],
                                       ps[:, s:s + 2, :].rearrange("p c n -> p (c n)")[:, 512 - n_off:640 + extra],
                                       ACT.Exp, bias=neg_max[:, U % 3:U % 3 + 1],
                                       accum_out=row_sum[:, U % 3:U % 3 + 1]).then_inc(exp_ready, 1)
                    if i >= 11 and (i - 11) % 8 == 0:
                        pair_squares(L, g, (i - 11) // 8)
                pair_squares(L, g, 3)

            def pair_squares(L, g, p):
                act.wait_ge(o_copied, L * 8 + g * 4 + p + 1)
                square(oT[:, 4 * g + p, first(L):], L, ST_SWA + g, p, first(L))

            def meta_attention(L, g):
                w = N_META + (1 if g == 0 else 0)
                act.wait_ge(m_dve, 20 * L + 10 * g + 4)
                act.activation(ms[:, :, 0:w], ms[:, :, 0:w], ACT.Exp).then_inc(m_exp, 1)

            hi(0)
            for m in range(KT):
                if m == 0:
                    act.wait_ge(consts_landed, 16)
                act.wait_ge(h_landed[m], 16)
                gained(m, gn[:, G_ATTN + m:G_ATTN + m + 1], 0)
                square(h[:, m, :], 0, ST_ATTN, m)
                if m == 3:
                    hi(1)
            for L in range(DEPTH):
                n0, f = unit0(L), first(L)
                gl = L * G_LAYER
                hi(n0 + 2)
                root(L, ST_ATTN, r_main)
                hi(n0 + 3)
                latent(L, 0, ST_KV, 0)
                hi(n0 + 4)
                latent(L, 1, ST_Q, 0)
                hi(n0 + 5)
                latent(L, 2, ST_Q, 1)
                root(L, ST_KV, r_kv)
                act.wait_ge(drained, acc0(L) + drain_rank("KRS"))
                act.activation(k_mla[64:P, :, :], kr_sum[64:P, :].unsqueeze(1).broadcast_to([64, HEADS, T]),
                               ACT.Copy).then_inc(krope_ready, 1)
                hi(n0 + 6)
                swap(L, "ka", 1.0, None)
                hi(n0 + 7)
                root(L, ST_Q, r_q)
                for j in range(4):
                    hi(n0 + 8 + j)
                    swap(L, f"q{j}", SWA_SCALE, "ka" if j == 0 else f"q{j - 1}")
                hi(n0 + 12)
                hi(n0 + 13)
                hi(n0 + 14)
                for g in range(2):
                    if L < DEPTH - 1:
                        meta_attention(L, g)
                    attention(L, g)
                    root(L, ST_SWA + g, r_kv if g == 0 else r_q, f)
                for t in range(KT):
                    act.wait_ge(mixf_ready, L * KT + t + 1)
                    act.activation(mix_hi[:, t, f:], oT[:, t, f:], ACT.Copy).then_inc(mixh_ready, 1)
                for m in range(KT):
                    hi(n0 + U_O + m + 2)
                    act.wait_ge(drained, acc0(L) + A_O + m + 1)
                    gained(m, gn[:, gl + G_FFN + m:gl + G_FFN + m + 1], f)
                    square(h[:, m, f:], L, ST_FFN, m, f)

                def silu(p, step=0):
                    act.wait_ge(drained, step * 2 + (acc0(L) + A_F + 2 * p + 2))
                    act.activation(gate[:, p % 2, f:], gate[:, p % 2, f:], ACT.Silu).then_inc(silu_done, 1)

                def act_part(p, at_tile, step=0):
                    act.wait_ge(prod_ready, step + (L * FT + p + 1))
                    if not isinstance(at_tile, int):
                        act.nop(nofuse=True)
                    act.activation(act_hi[:, at_tile, f:], up[:, p % 2, f:], ACT.Copy).then_inc(acth_ready, 1)

                for p in range(2):
                    hi(n0 + U_GU + 2 * p + 2)
                    if p == 0:
                        root(L, ST_FFN, r_main, f)
                    silu(p)
                    hi(n0 + U_GU + 2 * p + 3)
                    act_part(p, p)
                with act.Fori(0, FT // 2 - 1) as i:
                    for c in range(2):
                        hi(n0 + U_GU + 2 * c + 6, it=i)
                        silu(c + 2, step=i * 2)
                        hi(n0 + U_GU + 2 * c + 7, it=i)
                        act_part(c + 2, i * 2 + c + 2, step=i * 2)

                def down(m, step=0, at_m=None, last=False):
                    at_m = m if at_m is None else at_m
                    for c in range(4):
                        n = n0 + U_DOWN + 4 * m + 2 + c
                        if last and c >= 2:
                            if L == DEPTH - 1:
                                continue
                            hi(n)
                            continue
                        hi(n, P * DOWN_PARTS[(2 + c) % 4], it=step)
                    act.wait_ge(drained, step + (acc0(L) + A_D + m + 1))
                    if not isinstance(at_m, int):
                        act.nop(nofuse=True)
                    if L < DEPTH - 1:
                        gained(at_m, gn[:, bass.ds(at_m + (gl + G_LAYER + G_ATTN), 1)] if at_m is not m else
                               gn[:, gl + G_LAYER + G_ATTN + m:gl + G_LAYER + G_ATTN + m + 1], 0)
                    square(h[:, at_m, f:], L + 1, 0, m, f, step=step)

                with act.Fori(0, KT - 1) as i:
                    down(0, step=i, at_m=i)
                down(KT - 1, last=True)
            root(DEPTH, 0, r_main, N_META)

        @block.vector
        def _(dve):
            def lo(n, width=UNIT, it=0):
                dve.wait_ge(hi_ready, it * 4 + (n + 1))
                dve.tensor_tensor(w_lo[:, n % SPLIT, 0:width], raw[:, n % RAW, 0:width],
                                  f32(w_hi[:, n % SPLIT, 0:width]), ALU.subtract).then_inc(lo_ready, 1)

            def u_part(m, gain, f, n, step=0, at_m=None):
                at_m = m if at_m is None else at_m
                dve.wait_ge(uh_ready, step + (n + 1))
                dve.scalar_tensor_tensor(out=u_lo[:, at_m, f:], in0=h[:, at_m, f:], scalar=gain,
                                         in1=f32(u_hi[:, at_m, f:]), op0=ALU.mult, op1=ALU.subtract)\
                   .then_inc(u_ready, 1)

            def mean_square(L, k, a, slot, count, f_layer, rank=None):
                s = stat(L, k)
                v = tok_view(var[:, :], f_layer)
                rank = a + 1 if rank is None else rank
                dve.wait_ge(acc_ready, a + 1)
                if s:
                    dve.wait_ge(r_ready, s)
                dve.tensor_scalar(v, acc_view(slot, f_layer), 1.0 / count, EPS, ALU.mult, ALU.add)\
                   .then_inc(drained, 1)
                dve.wait_ge(drained, rank)
                dve.reciprocal(v, v).then_inc(var_ready, 1)

            def two(ap):
                return ap.rearrange("p (c n) -> p c n", c=2)

            def proj_wait(L, name):
                a = PROJ.index(name)
                dve.wait_ge(acc_ready, acc0(L) + a + 1)
                return a % 4

            def bank(s, lo_=0, hi_=P):
                return ps[lo_:hi_, 2 * s:2 * s + 2, 0:CHUNK]

            def scaled(L, name, dst, table, lo_=0, hi_=P):
                s = proj_wait(L, name)
                return dve.tensor_tensor(two(dst), bank(s, lo_, hi_), two(table), ALU.mult)

            def rotate(L, name, dst, scale, j):
                s = proj_wait(L, name)
                dve.wait_ge(swap_ready, 5 * L + j + 1)
                if L or j:
                    dve.wait_ge(drained, acc0(L) + drain_rank(name) - 1)
                dve.scalar_tensor_tensor(out=two(rot_a[:, :]), in0=bank(s), scalar=scale,
                                         in1=two(cos_r[:, :]), op0=ALU.mult, op1=ALU.mult).then_inc(rot_step, 1)
                dve.tensor_tensor(rot_b[:, :], swapped[:, :], sin_r[:, :], ALU.mult).then_inc(rot_step, 1)
                dve.wait_ge(rot_step, 2 * (5 * L + j) + 2)
                dve.tensor_tensor(dst, rot_a[:, :], rot_b[:, :], ALU.add).then_inc(drained, 1)

            def c_part(L, j):
                g = gn[:, L * G_LAYER + (G_KV if j == 0 else G_Q + j - 1):][:, 0:1]
                dve.wait_ge(ch_ready, 3 * L + j + 1)
                dve.scalar_tensor_tensor(out=c_lo[:, j, :], in0=c_raw[:, j, :], scalar=g,
                                         in1=f32(c_hi[:, j, :]), op0=ALU.mult, op1=ALU.subtract)\
                   .then_inc(c_ready, 1)

            def values(L, name, dst, dst_meta):
                s = proj_wait(L, name)
                dve.tensor_copy(dst, ps[:, 2 * s, :].rearrange("p (b n) -> p b n", b=NB))
                dve.tensor_copy(dst_meta, ps[0:N_META, 2 * s + 1, 0:P]).then_inc(drained, 1)

            def meta_attention(L, g):
                n0 = 20 * L + 10 * g
                w = N_META + (1 if g == 0 else 0)
                mask = cst[0:N_META, C_MASK + P:C_MASK + P + N_META].unsqueeze(1)\
                    .broadcast_to([N_META, 4, N_META])
                dve.wait_ge(m_pe, 3 * (2 * L + g) + 1)
                for e in range(2):
                    s_four = ps[0:N_META, 6 + e, 0:P].rearrange("p (h n) -> p h n", h=4)[:, :, 0:N_META]
                    ins = dve.tensor_tensor(ms[:, 4 * e:4 * e + 4, 0:N_META], s_four, mask, ALU.add)
                ins.then_inc(m_dve, 1)
                sink = gn[0:N_META, L * G_LAYER + G_SINK:L * G_LAYER + G_SINK + HEADS]
                dve.tensor_copy(ms[:, :, N_META], sink).then_inc(m_dve, 1)
                dve.wait_ge(m_dve, n0 + 2)
                dve.tensor_reduce(mrow[:, 0, :], ms[:, :, 0:w], AX.X, ALU.max).then_inc(m_dve, 1)
                dve.wait_ge(m_dve, n0 + 3)
                dve.tensor_tensor(ms[:, :, 0:w], ms[:, :, 0:w],
                                  mrow[:, 0, :].unsqueeze(2).broadcast_to([N_META, HEADS, w]),
                                  ALU.subtract).then_inc(m_dve, 1)
                dve.wait_ge(m_exp, 2 * L + g + 1)
                dve.tensor_reduce(mrow[:, 1, :], ms[:, :, 0:w], AX.X, ALU.add).then_inc(m_dve, 1)
                dve.wait_ge(m_dve, n0 + 5)
                dve.reciprocal(mrow[:, 2, :], mrow[:, 1, :]).then_inc(m_dve, 1)
                dve.wait_ge(m_dve, n0 + 6)
                dve.tensor_tensor(ms[:, :, 0:N_META], ms[:, :, 0:N_META],
                                  mrow[:, 2, :].unsqueeze(2).broadcast_to([N_META, HEADS, N_META]),
                                  ALU.mult).then_inc(m_dve, 1)
                dve.wait_ge(m_pe, 3 * (2 * L + g) + 2)
                dve.tensor_copy(mpT[:, :], ps[0:N_META, 5, 0:HEADS * N_META]).then_inc(m_dve, 1)
                dve.wait_ge(m_pe, 3 * (2 * L + g) + 3)
                dve.tensor_copy(oT[:, 4 * g:4 * g + 4, 0:N_META],
                                ps[:, 6, 0:4 * N_META].rearrange("p (t n) -> p t n", t=4)).then_inc(m_dve, 2)

            def attention(L, g):
                base_u = L * 2 * GB + g * GB

                def row_max(i):
                    _, _, b, _, _ = BLOCKS[g * GB + i]
                    U = base_u + i
                    n_off = key_range(g, b)[1]
                    extra = 1 if g == 0 else 0
                    s = 2 * (U % 3)
                    dve.wait_ge(s_ready, U + 1)
                    if U >= 3:
                        dve.wait_ge(exp_ready, U - 2)
                    dve.tensor_reduce(neg_max[:, U % 3:U % 3 + 1],
                                      ps[:, s:s + 2, :].rearrange("p c n -> p (c n)")[:, 512 - n_off:640 + extra],
                                      AX.X, ALU.max, negate=True).then_inc(max_ready, 1)

                def normalise(i):
                    _, _, b, _, _ = BLOCKS[g * GB + i]
                    U = base_u + i
                    n_off = key_range(g, b)[1]
                    c = U % 3
                    dve.wait_ge(exp_ready, U + 1)
                    if U >= 3:
                        dve.wait_ge(p_ready, U - 2)
                    dve.reciprocal(inv_sum[:, c:c + 1], row_sum[:, c:c + 1]).then_inc(inv_ready, 1)
                    dve.wait_ge(inv_ready, U + 1)
                    cols = probs[:, c, 400 - n_off:400 + P]
                    dve.tensor_scalar(cols, cols, inv_sum[:, c:c + 1], None, ALU.mult).then_inc(p_ready, 1)

                def copy_pT_meta(i):
                    _, _, b, _, _ = BLOCKS[g * GB + i]
                    if not key_range(g, b)[3]:
                        return
                    U = base_u + i
                    dve.wait_ge(pT_done, U + 1)
                    if U >= 2:
                        dve.wait_ge(pv_done, U - 1)
                    dve.tensor_copy(pT_meta[:, U % 2, :], ps[0:N_META, 2 * (U % 3) + 1, 0:P])\
                       .then_inc(pTm_copied, 1)

                def copy_o(p):
                    PP = L * 8 + g * 4 + p
                    dve.wait_ge(pv_done, base_u + 8 * p + 8)
                    dve.tensor_copy(oT[:, 4 * g + p, N_META:], ps[:, 6 + PP % 2, :]).then_inc(o_copied, 1)

                for i in range(GB + 3):
                    if i >= 3:
                        copy_pT_meta(i - 3)
                    if i < GB:
                        row_max(i)
                    if 1 <= i <= GB:
                        normalise(i - 1)
                    if i >= 11 and (i - 11) % 8 == 0:
                        copy_o((i - 11) // 8)
                copy_o(3)

            lo(0)
            dve.wait_ge(consts_landed, 16)
            for m in range(KT):
                dve.wait_ge(h_landed[m], 16)
                u_part(m, gn[:, G_ATTN + m:G_ATTN + m + 1], 0, m)
                if m == 3:
                    lo(1)
            dve.wait_ge(consts_landed, 32)
            dve.tensor_copy(ident_r[:, :], ident).then_inc(masks_ready, 1)
            dve.tensor_copy(mask_r[:, :], cst[:, C_MASK:C_MASK + 2 * P]).then_inc(masks_ready, 1)
            for L in range(DEPTH):
                n0, a0, f = unit0(L), acc0(L), first(L)
                gl = L * G_LAYER
                mean_square(L, ST_ATTN, a0 + PROJ.index("S1"), 1, D_MODEL, 0, a0 + 1)
                lo(n0 + 2)
                dve.wait_ge(r_ready, stat(L, ST_ATTN) + 1)
                scaled(L, "kva", c_raw[:, 0, :], r_main[:, :]).then_inc(drained, 1)
                dve.tensor_tensor(tbl_r[64:P, :], tbl[64:P, :], r_main[64:P, :], ALU.mult).then_inc(tables_ready, 1)
                dve.tensor_tensor(cos_r[:, :], cos_t, r_main[:, :], ALU.mult).then_inc(tables_ready, 1)
                dve.tensor_tensor(sin_r[:, :], sin_t, r_main[:, :], ALU.mult).then_inc(tables_ready, 1)
                dve.wait_ge(tables_ready, 4 * L + 3)
                s = proj_wait(L, "kr")
                dve.tensor_tensor(two(kr_t[0:64, :]), bank(s, 0, 64), two(tbl_r[64:P, :]), ALU.mult)\
                   .then_inc(drained, 1)
                lo(n0 + 3)
                c_part(L, 0)
                scaled(L, "qa0", c_raw[:, 1, :], r_main[:, :]).then_inc(drained, 1)
                lo(n0 + 4)
                c_part(L, 1)
                scaled(L, "qa1", c_raw[:, 2, :], r_main[:, :]).then_inc(drained, 1)
                lo(n0 + 5)
                c_part(L, 2)
                mean_square(L, ST_KV, a0 + PROJ.index("Skv"), PROJ.index("Skv") % 4, KV_RANK, 0)
                s = proj_wait(L, "KRS")
                dve.tensor_copy(two(kr_sum[64:P, :]), bank(s, 64, P)).then_inc(drained, 1)
                lo(n0 + 6)
                dve.wait_ge(krope_ready, L + 1)
                rotate(L, "ka", k_swa[:, :], 1.0, 0)
                lo(n0 + 7)
                scaled(L, "va", vT_swa[:, :], r_main[:, :]).then_inc(drained, 1)
                mean_square(L, ST_Q, a0 + PROJ.index("Sq"), PROJ.index("Sq") % 4, Q_RANK, 0)
                for j in range(4):
                    lo(n0 + 8 + j)
                    rotate(L, f"q{j}", q_swa[:, j, :], SWA_SCALE, j + 1)
                dve.wait_ge(r_ready, stat(L, ST_Q) + 1)
                dve.scalar_tensor_tensor(out=tbl_r[:, :], in0=tbl, scalar=MLA_SCALE, in1=r_q[:, :],
                                         op0=ALU.mult, op1=ALU.mult).then_inc(tables_ready, 1)
                values(L, "VA", v_swa[:, :, :], v_swa_meta[:, :])

                def nope(j):
                    s = proj_wait(L, f"n{j}")
                    for e in range(2):
                        ins = dve.tensor_tensor(two(k_mla[0:64, 2 * j + e, :]), bank(s, 64 * e, 64 * e + 64),
                                                two(r_kv[64 * e:64 * e + 64, :]), ALU.mult)
                    ins.then_inc(drained, 1)

                for name in PROJ[PROJ.index("n0"):]:
                    if name[0] == "n":
                        nope(int(name[1]))
                    elif name[0] == "v":
                        scaled(L, name, vT_mla[:, int(name[1]), :], r_kv[:, :]).then_inc(drained, 1)
                    elif name[0] == "V":
                        j = int(name[2])
                        values(L, name, v_mla[:, :, P * j:P * j + P], v_mla_meta[:, P * j:P * j + P])
                    else:
                        j = int(name[1])
                        if j == 0:
                            dve.wait_ge(tables_ready, 4 * L + 4)
                        scaled(L, name, q_mla[:, j, :], tbl_r[:, :]).then_inc(drained, 1)
                    if name in ("v3", "H3", "H7"):
                        lo(n0 + {"v3": 12, "H3": 13, "H7": 14}[name])
                for g in range(2):
                    if L < DEPTH - 1:
                        meta_attention(L, g)
                    attention(L, g)
                    mean_square(L, ST_SWA + g, a0 + A_G + g, 0, 4 * P, L)
                for t in range(KT):
                    g, gain = t // 4, gn[:, gl + G_SWA + t:gl + G_SWA + t + 1]
                    if t % 4 == 0:
                        dve.wait_ge(r_ready, stat(L, ST_SWA + g) + 1)
                    rr = (r_kv, r_q)[g]
                    dve.scalar_tensor_tensor(out=oT[:, t, f:], in0=oT[:, t, f:], scalar=gain, in1=rr[:, f:],
                                             op0=ALU.mult, op1=ALU.mult).then_inc(mixf_ready, 1)
                    if t:
                        mix_part(dve, L, t - 1, f)
                mix_part(dve, L, KT - 1, f)

                def add_h(a, slot, m, hn, step=0, at_m=None):
                    at_m = m if at_m is None else at_m
                    dve.wait_ge(acc_ready, step + (a + 1))
                    hv = tok_view(h[:, at_m, :], L)
                    dve.tensor_tensor(hv, hv, acc_view(slot, L), ALU.add).then_inc(drained, 1)

                for m in range(KT):
                    lo(n0 + U_O + m + 2)
                    add_h(a0 + A_O + m, m % 4, m, 0)
                    if m:
                        ffn_u(dve, u_part, L, m - 1, f)
                ffn_u(dve, u_part, L, KT - 1, f)

                def scale_acc(a, slot, dst, step=0):
                    dve.wait_ge(acc_ready, step + (a + 1))
                    dve.tensor_tensor(tok_view(dst, L), acc_view(slot, L), tok_view(r_main[:, :], L), ALU.mult)\
                       .then_inc(drained, 1)

                def act_part(p, tile, step=0):
                    dve.wait_ge(acth_ready, step + (L * FT + p + 1))
                    dve.tensor_tensor(act_lo[:, tile, f:], up[:, p % 2, f:], f32(act_hi[:, tile, f:]),
                                      ALU.subtract).then_inc(act_ready, 1)

                a1 = a0 + A_F
                mean_square(L, ST_FFN, a1 + 1, 1, D_MODEL, L, a1 + 1)
                for p in range(2):
                    lo(n0 + U_GU + 2 * p + 2)
                    if p == 0:
                        dve.wait_ge(r_ready, stat(L, ST_FFN) + 1)
                    i_gate, i_up = (0, 2) if p == 0 else (3, 4)
                    scale_acc(a1 + i_gate, i_gate % 4, gate[:, p, :])
                    if p:
                        act_part(p - 1, p - 1)
                    lo(n0 + U_GU + 2 * p + 3)
                    scale_acc(a1 + i_up, i_up % 4, up[:, p, :])
                with dve.Fori(0, FT // 2 - 1) as i:
                    for c in range(2):
                        p, j = c + 2, 5 + 2 * c
                        lo(n0 + U_GU + 2 * p + 2, it=i)
                        scale_acc(a1 + j, j % 4, gate[:, c, :], step=i * 4)
                        act_part(p - 1, i * 2 + (p - 1), step=i * 2)
                        lo(n0 + U_GU + 2 * p + 3, it=i)
                        scale_acc(a1 + j + 1, (j + 1) % 4, up[:, c, :], step=i * 4)
                act_part(FT - 1, FT - 1)

                a2 = a0 + A_D
                u0 = 2 * KT * L + 2 * KT

                def down(m, step=0, it=None, last=False):
                    for c in range(4):
                        n = n0 + U_DOWN + 4 * m + 2 + c
                        if last and c >= 2:
                            if L < DEPTH - 1:
                                lo(n)
                            continue
                        lo(n, P * DOWN_PARTS[(2 + c) % 4], it=step)
                    add_h(a2 + m, m % 2, m, 0, step=step, at_m=None if it is None else it)

                def next_u(m, step=0, at_m=None):
                    if L < DEPTH - 1:
                        gbase = gl + G_LAYER + G_ATTN
                        gain = gn[:, gbase + m:gbase + m + 1] if at_m is None else \
                            gn[:, bass.ds(at_m + gbase, 1)]
                        dve.wait_ge(drained, step + (a2 + m + 1))
                        u_part(m, gain, 0, u0 + m, step=step, at_m=at_m)

                down(0)
                down(1)
                next_u(0)
                with dve.Fori(0, KT // 2 - 2) as i:
                    for c in range(2):
                        down(c + 2, step=i * 2, it=i * 2 + (c + 2))
                        next_u(c + 1, step=i * 2, at_m=i * 2 + (c + 1))
                down(KT - 2)
                next_u(KT - 3)
                down(KT - 1, last=True)
                next_u(KT - 2)
                next_u(KT - 1)
            mean_square(DEPTH, 0, acc0(DEPTH), 2, D_MODEL, DEPTH - 1)
            dve.wait_ge(r_ready, stat(DEPTH, 0) + 1)
            for m in range(KT):
                dve.scalar_tensor_tensor(out=final[:, m, :], in0=h[:, m, N_META:], scalar=gn[:, G_FINAL + m:G_FINAL + m + 1],
                                         in1=r_main[:, N_META:], op0=ALU.mult, op1=ALU.mult).then_inc(final_ready, 1)

        @block.tensor
        def _(pe):
            def split_products(outs, n, tiles, rhs, begin, end):
                for x, (j, k, m_cols) in enumerate(tiles):
                    wh = w_hi[:, n % SPLIT, j:j + m_cols]
                    wl = w_lo[:, n % SPLIT, j:j + m_cols]
                    for y, (w, r) in enumerate(((wh, rhs[0]), (wh, rhs[1]), (wl, rhs[0]))):
                        for o, (c, cn) in outs:
                            mm = pe.matmul(o, w, r[:, k, c:c + cn], start=begin and x == 0 and y == 0,
                                           stop=end and x == len(tiles) - 1 and y == 2)
                return mm

            def acc_outs(slot, L, m_cols=P):
                return [(ps[0:m_cols, 2 * slot + c, 0:cn], (k, cn)) for c, (k, cn) in enumerate(chunks(L))]

            def ones_product(slot, L, f):
                for o, (c, cn) in acc_outs(slot, L):
                    mm = pe.matmul(o, ones, sq_sum[:, c:c + cn], start=True, stop=True)
                return mm

            def statistics(L, k, slot, f_layer):
                pe.wait_ge(sq_added, added0(L, k) + STAT_TILES[k] + 1 if k or L < DEPTH else
                           added0(DEPTH, 0) + KT + 1)
                ones_product(slot, f_layer, 0).then_inc(acc_ready, 1)

            def project(L):
                n0, a0 = unit0(L), acc0(L)

                for a, name in enumerate(PROJ):
                    slot = a % 4
                    if a >= 4:
                        pe.wait_ge(drained, a0 + max(drain_rank(x) for x in PROJ[:a - 3]))
                    if name in UNIT_OF:
                        n = n0 + UNIT_OF[name]
                        pe.wait_ge(lo_ready, n + 1)
                        cols = 64 if name == "kr" else P
                        outs = acc_outs(slot, 0, cols)
                        for k in range(KT):
                            if name == "kva":
                                pe.wait_ge(u_ready, 2 * KT * L + k + 1)
                            mm = split_products(outs, n, [(k * P, k, cols)], (u_hi, u_lo), k == 0, k == KT - 1)
                        mm.then_inc(acc_ready, 1)
                    elif name in ("S1", "Skv", "Sq"):
                        if a == 1 and L == 0:
                            pe.wait_ge(consts_landed, 32)
                        statistics(L, {"S1": ST_ATTN, "Skv": ST_KV, "Sq": ST_Q}[name], slot, 0)
                    elif name == "KRS":
                        pe.wait_ge(drained, a0 + drain_rank("kr"))
                        for c in range(2):
                            mm = pe.matmul(ps[64:P, 2 * slot + c, 0:CHUNK], sel,
                                           kr_t[0:64, c * CHUNK:(c + 1) * CHUNK], start=True, stop=True)
                        mm.then_inc(acc_ready, 1)
                    elif name[0] == "V":
                        src = vT_swa[:, :] if name == "VA" else vT_mla[:, int(name[2]), :]
                        pe.wait_ge(drained, a0 + drain_rank("va" if name == "VA" else f"v{name[2]}"))
                        for b in range(NB):
                            pe.transpose(ps[:, 2 * slot, P * b:P * b + P],
                                         src[:, N_META + P * b:N_META + P * b + P], ident)
                        pe.transpose(ps[0:N_META, 2 * slot + 1, 0:P], src[:, 0:N_META], ident)\
                          .then_inc(acc_ready, 1)
                    elif name[0] in "nv":
                        j = int(name[1]) + (4 if name[0] == "v" else 0)
                        n = n0 + U_KV
                        if j == 0:
                            pe.wait_ge(lo_ready, n + 1)
                            pe.wait_ge(c_ready, 3 * L + 1)
                        mm = split_products(acc_outs(slot, 0), n, [(j * P, 0, P)], (c_hi, c_lo), True, True)
                        mm.then_inc(acc_ready, 1)
                    else:
                        j = int(name[1])
                        n = n0 + U_Q + j // 4
                        if j % 4 == 0:
                            pe.wait_ge(lo_ready, n + 1)
                            pe.wait_ge(c_ready, 3 * L + 3)
                        at_ = (j % 4) * 2 * P
                        mm = split_products(acc_outs(slot, 0), n, [(at_, 1, P), (at_ + P, 2, P)],
                                            (c_hi, c_lo), True, True)
                        mm.then_inc(acc_ready, 1)

            def q_rows(g, head, c0, cn):
                if g == 0:
                    r = 64 * (head // 4)
                    return q_swa[r:r + 64, head % 4, c0:c0 + cn]
                return q_mla[:, head, c0:c0 + cn]

            def k_rows(g, head, c0, cn):
                if g == 0:
                    r = 64 * (head // 4)
                    return k_swa[r:r + 64, c0:c0 + cn]
                return k_mla[:, head, c0:c0 + cn]

            def v_rows(g, head, b):
                c = 64 * (head // 4) if g == 0 else 64 * head
                if b is None:
                    return (v_swa_meta if g == 0 else v_mla_meta)[:, c:c + 64]
                return (v_swa if g == 0 else v_mla)[:, b, c:c + 64]

            def meta_attention(L, g):
                c0 = 20 * L + 10 * g
                for head in range(HEADS):
                    mm = pe.matmul(ps[0:N_META, 6 + head // 4, 32 * (head % 4):32 * (head % 4) + N_META], q_rows(g, head, 0, N_META),
                                   k_rows(g, head, 0, N_META), start=True, stop=True)
                mm.then_inc(m_pe, 1)
                pe.wait_ge(m_dve, c0 + 7)
                for head in range(HEADS):
                    mm = pe.transpose(ps[0:N_META, 5, N_META * head:N_META * head + N_META],
                                      ms[:, head, 0:N_META], cst[0:N_META, C_ID:C_ID + N_META])
                mm.then_inc(m_pe, 1)
                pe.wait_ge(m_dve, c0 + 8)
                for head in range(HEADS):
                    p, half = (head % 4, head // 4) if g == 0 else (head // 2, head % 2)
                    mm = pe.matmul(ps[64 * half:64 * half + 64, 6, N_META * p:N_META * p + N_META],
                                   v_rows(g, head, None), mpT[:, N_META * head:N_META * head + N_META],
                                   start=True, stop=True)
                mm.then_inc(m_pe, 1)
                pe.wait_ge(m_dve, c0 + 10)

            def attention(L, g):
                base_u = L * 2 * GB + g * GB

                def scores(i):
                    _, head, b, _, _ = BLOCKS[g * GB + i]
                    U = base_u + i
                    s = 2 * (U % 3)
                    k0, n_off, _, _ = key_range(g, b)
                    if i >= 3:
                        _, _, bb, _, _ = BLOCKS[g * GB + i - 3]
                        pe.wait_ge(pT_copied, U - 2)
                        if key_range(g, bb)[3]:
                            pe.wait_ge(pTm_copied, metas(L, g, i - 2))
                    q = q_rows(g, head, N_META + P * b, P)
                    pe.matmul(ps[:, s, 512 - n_off:512], q, k_rows(g, head, k0, n_off), start=True, stop=g == 1)
                    if g == 0:
                        pe.matmul(ps[:, s, 512 - n_off:512], ident_r[:, :], mask_r[:, P - n_off:P],
                                  start=False, stop=True)
                    pe.matmul(ps[:, s + 1, 0:P], q, k_rows(g, head, N_META + P * b, P), start=True, stop=False)
                    mm = pe.matmul(ps[:, s + 1, 0:P], ident_r[:, :], mask_r[:, P:2 * P], start=False, stop=True)
                    if g == 0:
                        c = L * G_LAYER + G_SINK + head
                        mm = pe.matmul(ps[:, s + 1, P:P + 1], ident, gn[:, c:c + 1], start=True, stop=True)
                    mm.then_inc(s_ready, 1)

                def turn(i):
                    _, _, b, _, _ = BLOCKS[g * GB + i]
                    U = base_u + i
                    s = 2 * (U % 3)
                    _, n_off, blocks, meta = key_range(g, b)
                    pe.wait_ge(p_ready, U + 1)
                    c0 = 400 - n_off
                    if meta:
                        pe.transpose(ps[0:N_META, s + 1, 0:P], probs[:, U % 3, c0:c0 + N_META], ident)
                        c0 += N_META
                    for x in range(len(blocks) + 1):
                        mm = pe.transpose(ps[:, s, P * x:P * x + P], probs[:, U % 3, c0 + P * x:c0 + P * x + P],
                                          ident)
                    mm.then_inc(pT_done, 1)

                def outputs(i):
                    _, head, b, p, half = BLOCKS[g * GB + i]
                    U = base_u + i
                    PP = L * 8 + g * 4 + p
                    _, _, blocks, meta = key_range(g, b)
                    pe.wait_ge(pT_copied, U + 1)
                    if half == 0 and b == 0 and PP >= 2:
                        pe.wait_ge(o_copied, PP - 1)
                    o = ps[64 * half:64 * half + 64, 6 + PP % 2, P * b:P * b + P]
                    if meta:
                        pe.wait_ge(pTm_copied, metas(L, g, i + 1))
                        pe.matmul(o, v_rows(g, head, None), pT_meta[:, U % 2, :], start=True, stop=False)
                    todo = blocks + [b]
                    for x, kb in enumerate(todo):
                        mm = pe.matmul(o, v_rows(g, head, kb), pT[:, U % 2, P * x:P * x + P],
                                       start=x == 0 and not meta, stop=x == len(todo) - 1)
                    mm.then_inc(pv_done, 1)

                for i in range(GB + 3):
                    if i < GB:
                        scores(i)
                    if i >= 3:
                        outputs(i - 3)
                    if 2 <= i < GB + 2:
                        turn(i - 2)

            def metas(L, g, upto):
                per = [sum(key_range(x, b)[3] for _, _, b, _, _ in BLOCKS[x * GB:(x + 1) * GB]) for x in range(2)]
                own = sum(key_range(g, b)[3] for _, _, b, _, _ in BLOCKS[g * GB:g * GB + upto])
                return L * sum(per) + (per[0] if g else 0) + own

            for L in range(DEPTH):
                n0, a0 = unit0(L), acc0(L)
                project(L)
                pe.wait_ge(drained, a0 + A_G)
                pe.wait_ge(masks_ready, 2)
                pe.wait_ge(krope_ready, L + 1)
                for g in range(2):
                    if L < DEPTH - 1:
                        meta_attention(L, g)
                    attention(L, g)
                    statistics(L, ST_SWA + g, 0, L)
                    pe.wait_ge(drained, a0 + A_G + g + 1)

                def unit(n, slot, tiles, rhs, begin, end, step=0):
                    pe.wait_ge(lo_ready, step + (n + 1))
                    split_products(acc_outs(slot, L), n, tiles, rhs, begin, end)\
                        .then_inc(acc_ready if end else unit_used, 1)

                whole = [(k * P, k, P) for k in range(KT)]
                for m in range(KT):
                    n, slot = n0 + U_O + m, m % 4
                    if m >= 4:
                        pe.wait_ge(drained, a0 + A_O + m - 3)
                    if m == 0:
                        pe.wait_ge(lo_ready, n + 1)
                        for k in range(KT):
                            pe.wait_ge(mix_ready, L * KT + k + 1)
                            mm = split_products(acc_outs(slot, L), n, [whole[k]], (mix_hi, mix_lo), k == 0, k == KT - 1)
                        mm.then_inc(acc_ready, 1)
                    else:
                        unit(n, slot, whole, (mix_hi, mix_lo), True, True)
                a1 = a0 + A_F
                pe.wait_ge(drained, a1)
                for j, i_acc in enumerate((0, 2, 3, 4)):
                    if j == 0:
                        pe.wait_ge(lo_ready, n0 + U_GU + 1)
                        for k in range(KT):
                            pe.wait_ge(u_ready, 2 * KT * L + KT + k + 1)
                            mm = split_products(acc_outs(0, L), n0 + U_GU, [whole[k]], (u_hi, u_lo), k == 0,
                                                k == KT - 1)
                        mm.then_inc(acc_ready, 1)
                        statistics(L, ST_FFN, 1, L)
                        continue
                    if i_acc == 4:
                        pe.wait_ge(drained, a1 + 2)
                    unit(n0 + U_GU + j, i_acc % 4, whole, (u_hi, u_lo), True, True)
                with pe.Fori(0, FT // 2 - 1) as i:
                    for c in range(4):
                        pe.wait_ge(drained, i * 4 + (a1 + 5 + c - 3))
                        unit(n0 + U_GU + 4 + c, (5 + c) % 4, whole, (u_hi, u_lo), True, True, step=i * 4)
                a2 = a0 + A_D
                pe.wait_ge(drained, a2)
                with pe.Fori(0, KT // 2) as i:
                    for c in range(2):
                        pe.wait_ge(drained, i * 2 + (a2 + c - 1))
                        for x, (k0, kn) in enumerate(zip(DOWN_AT, DOWN_PARTS)):
                            pe.wait_ge(act_ready, L * FT + k0 + kn)
                            unit(n0 + U_DOWN + 4 * c + x, c, [(k * P, k0 + k, P) for k in range(kn)],
                                 (act_hi, act_lo), x == 0, x == 3, step=i * 8)
            statistics(DEPTH, 0, 2, DEPTH - 1)


def _tables():
    pos = np.arange(T, dtype=np.float32)

    def angles(d):
        inv = np.float32(10000.0) ** (-np.arange(0, d, 2, dtype=np.float32) / np.float32(d))
        return inv.astype(np.float32)[:, None] * pos[None, :]

    a, b = angles(SWA_DIM), angles(ROPE)
    cos_a = np.concatenate([np.cos(a)] * 4)
    sin_a = np.concatenate([-np.sin(a), np.sin(a)] * 2)
    tbl = np.concatenate([np.ones((NOPE, T)), np.cos(b), np.cos(b), -np.sin(b), np.sin(b)])
    ident = np.eye(P)
    ones = np.ones((P, P))
    sel = np.zeros((P, 64))
    for j in range(64):
        sel[j % 32, j] = sel[32 + j % 32, j] = 1.0
    r, c = np.arange(P)[:, None], np.arange(P)[None, :]
    prev, cur = np.where(c > r, 0.0, NEG), np.where(c <= r, 0.0, NEG)
    return np.concatenate([ident, ones, sel, prev, cur, cos_a, sin_a, tbl], axis=1).astype(np.float32)


def _orders():
    q, k = np.arange(512), 512 + np.arange(128)
    v, qa = 640 + np.arange(128), 768 + np.arange(256)
    kva, kr = 1024 + np.arange(128), 1152 + np.arange(32)
    heads = q.reshape(HEADS, SWA_DIM)
    q_tiles = np.concatenate([np.concatenate([heads[t], heads[t + 4]]) for t in range(4)])
    swap = np.concatenate([np.arange(16, 32), np.arange(16)])
    w_in = np.concatenate([kva, kr, kr[swap], np.zeros(64, int), qa, k, v, q_tiles])
    kv = np.arange(HEADS * 128).reshape(HEADS, 128)
    w_kv = np.concatenate([kv[:, :NOPE].ravel(), kv[:, NOPE:].ravel()])
    qu = np.arange(HEADS * 96).reshape(HEADS, 96)
    w_q = np.concatenate([qu, qu[:, NOPE:][:, swap]], axis=1).ravel()
    return w_in, w_kv, w_q, q_tiles


def _tiles(w, k_tiles):
    L, K, M = w.shape
    return w.reshape(L, k_tiles, P, M // P, P).transpose(0, 3, 2, 1, 4)


def _columns(g):
    return g.reshape(-1, P).T


def kernel(x, meta_tokens, attn_norm, w_in, q_norm, w_q_up, kv_norm, w_kv_up, sinks,
           out_norm_swa, out_norm_mla, w_o, ffn_norm, w_gate, w_up, w_down, final_norm):
    import concourse.bacc as bacc
    from concourse.bass_utils import run_bass_kernel_spmd

    o_in, o_kv, o_q, q_tiles = _orders()
    tokens = np.concatenate([np.asarray(meta_tokens), np.asarray(x)[0]], axis=0)
    w_o = np.asarray(w_o)
    w_o = np.concatenate([w_o[:, q_tiles], w_o[:, 512:]], axis=1)
    gains = []
    for l in range(DEPTH):
        gains += [_columns(np.asarray(attn_norm)[l]), _columns(np.asarray(ffn_norm)[l]),
                  _columns(np.asarray(q_norm)[l]), _columns(np.asarray(kv_norm)[l]),
                  _columns(np.asarray(out_norm_swa)[l][q_tiles]), _columns(np.asarray(out_norm_mla)[l]),
                  np.broadcast_to(np.asarray(sinks)[l][None, :], (P, HEADS))]
    gains.append(_columns(np.asarray(final_norm)))
    arrays = {
        "tokens_t": tokens.T.reshape(KT, P, T),
        "constants": _tables(),
        "gains": np.concatenate(gains, axis=1),
        "w_in_t": _tiles(np.asarray(w_in)[:, :, o_in], KT).reshape(DEPTH, 10, P, UNIT),
        "w_kv_t": np.asarray(w_kv_up)[:, :, o_kv],
        "w_q_t": _tiles(np.asarray(w_q_up)[:, :, o_q], 2).reshape(DEPTH, 2, 4, P, 2 * P)
            .transpose(0, 1, 3, 2, 4).reshape(DEPTH, 2, P, UNIT),
        "w_o_t": _tiles(w_o, KT).reshape(DEPTH, KT, P, UNIT),
        "w_gate_t": _tiles(np.asarray(w_gate), KT).reshape(DEPTH, FT, P, UNIT),
        "w_up_t": _tiles(np.asarray(w_up), KT).reshape(DEPTH, FT, P, UNIT),
        "w_down_t": _tiles(np.asarray(w_down), FT).reshape(DEPTH, KT, P, FT * P),
    }
    arrays = {k: np.ascontiguousarray(a) for k, a in arrays.items()}
    nc = bacc.Bacc("TRN2", target_bir_lowering=False, num_devices=1)
    args = [nc.dram_tensor(k, a.shape, mybir.dt.from_np(a.dtype), kind="ExternalInput").ap()
            for k, a in arrays.items()]
    args.append(nc.dram_tensor("out_t", (KT, P, SEQ), F32, kind="ExternalOutput").ap())
    build(nc, *args)
    r = run_bass_kernel_spmd(nc, [arrays], core_ids=[0])
    return np.ascontiguousarray(np.asarray(r.results[0]["out_t"]).reshape(D_MODEL, SEQ).T)[None]
```

```python
from contextlib import ExitStack

import numpy as np

import concourse.bass as bass
from concourse import mybir

F32 = mybir.dt.float32
F32R = mybir.dt.float32r
ALU = mybir.AluOpType
ACT = mybir.ActivationFunctionType
AX = mybir.AxisListType

P = 128
D_MODEL = 1024
DEPTH = 2
N_META = 16
SEQ = 512
T = N_META + SEQ
NB = SEQ // P
EPS = 1e-6
NEG = -1e30
HEADS = 8
SWA_DIM = 64
Q_RANK = 256
KV_RANK = 128
NOPE = 64
ROPE = 32
V_DIM = 64
SWA_SCALE = SWA_DIM ** -0.5
MLA_SCALE = (NOPE + ROPE) ** -0.5
D_FF = -(-8 * D_MODEL // (3 * 256)) * 256
KT = D_MODEL // P
FT = D_FF // P
UNIT = KT * P
CHUNK = T // 2

U_IN, U_KV, U_Q, U_O, U_GU, U_DOWN = 0, 10, 11, 13, 21, 21 + 2 * FT
DOWN_PARTS = (6, 6, 5, 5)
DOWN_AT = (0, 6, 12, 17)
UNITS = U_DOWN + KT * len(DOWN_PARTS)
RAW, SPLIT = 4, 2
O_UNITS = [(0, 0), (2, 0), (0, 1), (2, 1), (4, 0), (6, 0), (4, 1), (6, 1)]
S_RING, PT_BANK, O_BANK = 4, 5, 7
S_LONG = 512 - (T - P)
STAT_AT, ROOT_AT, MIX_AT = 42, 47, 49

PROJ = ["kva", "S1", "kr", "qa0", "qa1", "Skv", "KRS", "ka", "va", "Sq", "q0", "q1", "q2", "q3", "VA",
        "n0", "n1", "n2", "n3", "v0", "v1", "VT0", "v2", "VT1", "v3", "VT2", "H0", "VT3",
        "H1", "H2", "H3", "H4", "H5", "H6", "H7"]
DRAIN = ["S1", "kva"] + PROJ[2:]
UNIT_OF = {"kva": 0, "kr": 1, "qa0": 2, "qa1": 3, "ka": 4, "va": 5, "q0": 6, "q1": 7, "q2": 8, "q3": 9}
A_G = len(PROJ)
A_O = A_G + 2
A_F = A_O + KT
A_D = A_F + 2 * FT + 1
ACCS = A_D + KT
STAT_TILES = [KT, 1, 2, 4, 4, KT]
ST_ATTN, ST_KV, ST_Q, ST_SWA, ST_MLA, ST_FFN = range(6)
STATS = len(STAT_TILES)

C_ID, C_ONES, C_SEL, C_MASK, C_COS, C_SIN, C_TBL = 0, 128, 256, 320, 576, 576 + T, 576 + 2 * T
C_END = 576 + 3 * T
G_ATTN, G_FFN, G_Q, G_KV, G_SWA, G_MLA, G_SINK, G_LAYER = 0, 8, 16, 18, 19, 23, 27, 35
G_FINAL = DEPTH * G_LAYER


def build(nc, xT, consts, gains, w_in, w_kv, w_q, w_o, w_gate, w_up, w_down, out):
    ctx = ExitStack()
    with ctx:
        base = nc.sbuf_base
        at = [-(-base // 64) * 64]

        def place(name, shape, dt=F32, offset=None):
            size = 4 * int(np.prod(shape[1:]))
            if offset is None:
                offset = at[0]
                at[0] += -(-size // 32) * 32
            return nc.alloc_sbuf_tensor_at(name, shape, dt, offset=offset)

        def sem(name):
            return ctx.enter_context(nc.semaphore(name))

        h = place("h", [P, KT, T])
        u_hi = place("u_hi", [P, KT, T], F32R)
        u_lo = place("u_lo", [P, KT, T], F32R)
        raw = place("raw", [P, RAW, UNIT])
        w_hi = place("w_hi", [P, SPLIT, UNIT], F32R)
        w_lo = place("w_lo", [P, SPLIT, UNIT], F32R)
        x0 = at[0]
        act_hi = place("act_hi", [P, FT, T], F32R)
        act_lo = place("act_lo", [P, FT, T], F32R)
        x1 = at[0]
        at[0] = x0
        q_swa = place("q_swa", [P, 4, T])
        k_swa = place("k_swa", [P, T])
        v_swa = place("v_swa", [P, NB, P])
        v_swa_meta = place("v_swa_meta", [N_META, P])
        mix_at = at[0]
        q_mla = place("q_mla", [P, HEADS, T])
        k_mla = place("k_mla", [P, HEADS, T])
        mix_hi_a = place("mix_hi_a", [P, 4, T], F32R, offset=x0)
        mix_hi_b = place("mix_hi_b", [P, 4, T], F32R, offset=mix_at)
        mix_lo_b = place("mix_lo_b", [P, 4, T], F32R, offset=mix_at + 4 * KT * T)
        v_mla = place("v_mla", [P, NB, HEADS * V_DIM])
        v_mla_meta = place("v_mla_meta", [N_META, HEADS * V_DIM])
        soft_at = at[0]
        probs = place("probs", [P, S_RING, T + 1])
        pT = place("pT", [P, 2, P + NB * P])
        vT_mla = place("vT_mla", [P, 4, T], offset=soft_at)
        vT_swa = place("vT_swa", [P, T], offset=soft_at + 4 * 4 * T)
        o_at = at[0]
        oT = place("oT", [P, 8, T])
        c_hi = place("c_hi", [P, 3, T], F32R, offset=o_at)
        c_lo = place("c_lo", [P, 3, T], F32R, offset=o_at + 4 * 3 * T)
        sin_r = place("sin_r", [P, T], offset=o_at + 4 * 6 * T)
        cos_r = place("cos_r", [P, T], offset=o_at + 4 * 7 * T)
        r_kv = place("r_kv", [P, T])
        assert at[0] <= x1, (at[0], x1)
        at[0] = max(at[0], x1)
        cst = place("cst", [P, C_END])
        gn = place("gn", [P, G_FINAL + KT])
        ident_r = place("ident_r", [P, P], F32R)
        mask_r = place("mask_r", [P, 2 * P], F32R)
        r_main = place("r_main", [P, T])
        r_q = place("r_q", [P, T])
        tbl_r = place("tbl_r", [P, T])
        var = place("var", [P, T])
        sq = place("sq", [P, T])
        sq_sum = place("sq_sum", [P, T])
        z = at[0]
        c_raw = place("c_raw", [P, 3, T])
        swapped = place("swapped", [P, T])
        rot_a = place("rot_a", [P, T])
        rot_b = place("rot_b", [P, T])
        mix_lo_a = place("mix_lo_a", [P, 4, T], F32R, offset=z + 2048)
        gate = place("gate", [P, 2, T], offset=z)
        up = place("up", [P, 2, T], offset=z + 8 * T)
        neg_max = place("neg_max", [P, S_RING])
        row_sum = place("row_sum", [P, S_RING])
        inv_sum = place("inv_sum", [P, S_RING])
        ms = place("ms", [N_META, HEADS, N_META + 1], offset=z)
        mrow = place("mrow", [N_META, 3, HEADS], offset=z + 640)
        mpT = place("mpT", [N_META, HEADS * N_META], offset=z + 768)
        assert at[0] <= nc.sbuf_usable_end, (at[0], nc.sbuf_usable_end)
        kr_t, kr_sum = rot_a, rot_b
        final = place("final", [P, KT, SEQ], offset=x0)

        ident = cst[:, C_ID:C_ID + P]
        ones = cst[:, C_ONES:C_ONES + P]
        sel = cst[0:64, C_SEL:C_SEL + 64]
        cos_t = cst[:, C_COS:C_COS + T]
        sin_t = cst[:, C_SIN:C_SIN + T]
        tbl = cst[:, C_TBL:C_TBL + T]

        ps = ctx.enter_context(nc.psum_tensor("ps", [P, 8, 512], F32))

        consts_landed = sem("consts_landed")
        h_landed = [sem(f"h_landed{k}") for k in range(KT)]
        raw_landed = [sem(f"raw_landed{k}") for k in range(RAW)]
        hi_ready = sem("hi_ready")
        lo_ready = sem("lo_ready")
        o_half_used = sem("o_half_used")
        unit_used = sem("unit_used")
        acc_ready = sem("acc_ready")
        drained = sem("drained")
        masks_ready = sem("masks_ready")
        uh_ready = sem("uh_ready")
        u_ready = sem("u_ready")
        sq_made = sem("sq_made")
        sq_added = sem("sq_added")
        var_ready = sem("var_ready")
        r_ready = sem("r_ready")
        tables_ready = sem("tables_ready")
        ch_ready = sem("ch_ready")
        c_ready = sem("c_ready")
        swap_ready = sem("swap_ready")
        rot_step = sem("rot_step")
        krope_ready = sem("krope_ready")
        s_ready = sem("s_ready")
        sink_put = sem("sink_put")
        max_ready = sem("max_ready")
        exp_ready = sem("exp_ready")
        inv_ready = sem("inv_ready")
        p_ready = sem("p_ready")
        pT_done = sem("pT_done")
        pT_copied = sem("pT_copied")
        pv_done = sem("pv_done")
        o_copied = sem("o_copied")
        m_pe = sem("m_pe")
        m_dve = sem("m_dve")
        m_exp = sem("m_exp")
        mixf_ready = sem("mixf_ready")
        mixh_ready = sem("mixh_ready")
        mix_ready = sem("mix_ready")
        silu_done = sem("silu_done")
        prod_ready = sem("prod_ready")
        acth_ready = sem("acth_ready")
        act_ready = sem("act_ready")
        final_ready = sem("final_ready")
        stored = sem("stored")

        def unit0(L):
            return L * UNITS

        def acc0(L):
            return L * ACCS

        def stat(L, k):
            return L * STATS + k

        def made0(L, k):
            return L * sum(STAT_TILES) + sum(STAT_TILES[:k])

        def added0(L, k):
            return made0(L, k) + stat(L, k)

        def stat_acc(L, k):
            names = {ST_ATTN: "S1", ST_KV: "Skv", ST_Q: "Sq"}
            if L == DEPTH:
                return acc0(DEPTH)
            return acc0(L) + (PROJ.index(names[k]) if k in names else A_G + k - ST_SWA if k < ST_FFN else A_F + 1)

        def wait_sum_read(eng, L, k):
            if stat(L, k):
                eng.wait_ge(acc_ready, (stat_acc(L, k - 1) if k else stat_acc(L - 1, STATS - 1)) + 1)

        def wait_used(eng, n, it=0):
            L, r = divmod(n, UNITS)
            if r >= U_DOWN:
                m, x = divmod(r - U_DOWN, 4)
                if x < 3:
                    eng.wait_ge(unit_used, it * 3 + (3 * (KT * L + m) + x + 1))
                else:
                    eng.wait_ge(acc_ready, it + (acc0(L) + A_D + m + 1))
                return
            if r >= U_GU:
                j = r - U_GU
                a = A_F + (j + 1 if j else 0)
            elif r >= U_O:
                m0, half = O_UNITS[r - U_O]
                if not half:
                    eng.wait_ge(o_half_used, 4 * L + sum(1 - y for _, y in O_UNITS[:r - U_O]) + 1)
                    return
                a = A_O + m0 + 1
            else:
                a = PROJ.index({U_KV: "v3", U_Q: "H3", U_Q + 1: "H7"}.get(r) or
                               next(k for k, u in UNIT_OF.items() if u == r))
            eng.wait_ge(acc_ready, it * 4 + (acc0(L) + a + 1))

        def first(L):
            return 0 if L < DEPTH - 1 else N_META

        def chunks(L):
            return [(0, CHUNK), (CHUNK, CHUNK)] if L < DEPTH - 1 else [(N_META, SEQ)]

        def acc_view(slot, L, lo=0, hi=P):
            if slot == "pT":
                return ps[lo:hi, PT_BANK:PT_BANK + 2, 0:CHUNK] if L < DEPTH - 1 else ps[lo:hi, PT_BANK, 0:SEQ]
            if L < DEPTH - 1:
                return ps[lo:hi, 2 * slot:2 * slot + 2, 0:CHUNK]
            return ps[lo:hi, 2 * slot, 0:SEQ]

        def tok_view(tile, L):
            if L < DEPTH - 1:
                return tile.rearrange("p (c n) -> p c n", c=2)
            return tile[:, N_META:T]

        def f32(ap):
            return ap.bitcast(F32)

        def drain_rank(name):
            return DRAIN.index(name) + 1

        def attn_blocks():
            for g in range(2):
                for p in range(4):
                    for half in range(2):
                        head = p + 4 * half if g == 0 else 2 * p + half
                        for b in range(NB):
                            yield g, head, b, p, half

        BLOCKS = list(attn_blocks())
        GB = len(BLOCKS) // 2

        def key_range(g, b):
            diag = N_META + P * b
            if g == 0 and b:
                return diag - P, 2 * P, [b - 1, b], False
            return 0, diag + P, list(range(b + 1)), True

        def s_view(g, b, n):
            if g and b == NB - 1:
                return ps[:, 3:5, :].rearrange("p c n -> p (c n)")[:, S_LONG:S_LONG + n]
            return ps[:, b, 0:n]

        def turned(U, x, w=1):
            g, _, b, _, _ = BLOCKS[U % len(BLOCKS)]
            if g and b == NB - 1:
                return ps[:, 4:6, :].rearrange("p c n -> p (c n)")[:, 512 - P + P * x:512 - P + P * (x + w)]
            return ps[:, PT_BANK + 1 - U % 2, P * x:P * (x + w)]

        def pieces(g, b):
            _, _, blocks, meta = key_range(g, b)
            return [0] * meta + [N_META * meta + P * x for x in range(len(blocks))]

        def mix_tile(part, t):
            if t < 4:
                return (mix_hi_a if part == "hi" else mix_lo_a)[:, t, :]
            return (mix_hi_b if part == "hi" else mix_lo_b)[:, t - 4, :]

        def mix_part(dve, L, t, f):
            dve.wait_ge(mixh_ready, L * KT + t + 1)
            dve.tensor_tensor(mix_tile("lo", t)[:, f:], oT[:, t, f:], f32(mix_tile("hi", t)[:, f:]), ALU.subtract)\
               .then_inc(mix_ready, 1)

        def ffn_u(dve, u_part, L, m, f):
            g = L * G_LAYER + G_FFN + m
            dve.wait_ge(drained, acc0(L) + A_O + m + 1)
            u_part(m, gn[:, g:g + 1], f, 2 * KT * L + KT + m)

        block = ctx.enter_context(nc.Block())

        @block.sync
        def _(sp):
            def load(n, src, width=UNIT, it=0):
                slot = n % RAW
                if n >= RAW:
                    sp.wait_ge(lo_ready, it * 4 + (n - RAW + 1))
                sp.dma_start(raw[:, slot, 0:width], src).then_inc(raw_landed[slot], 16)

            for k in range(KT):
                if k == 0:
                    sp.dma_start(gn[:, :], gains).then_inc(consts_landed, 16)
                sp.dma_start(h[:, k, :], xT[k]).then_inc(h_landed[k], 16)
                if k in (1, 4):
                    n = 0 if k == 1 else 1
                    load(n, w_in[0, n])
            sp.dma_start(cst[:, :], consts).then_inc(consts_landed, 16)
            for L in range(DEPTH):
                n0 = unit0(L)
                for j in range(2 if L == 0 else 0, 10):
                    load(n0 + j, w_in[L, j])
                load(n0 + U_KV, w_kv[L])
                for j in range(2):
                    load(n0 + U_Q + j, w_q[L, j])
                for j in range(KT):
                    load(n0 + U_O + j, w_o[L, j])
                with sp.Fori(0, FT // 2) as i:
                    for c in range(4):
                        w = w_gate if c % 2 == 0 else w_up
                        load(n0 + U_GU + c, w[L, i * 2 + c // 2], it=i)
                with sp.Fori(0, KT) as i:
                    for c, (k0, kn) in enumerate(zip(DOWN_AT, DOWN_PARTS)):
                        load(n0 + U_DOWN + c, w_down[L, i, :, k0 * P:(k0 + kn) * P], kn * P, it=i)
            for m in range(KT):
                sp.wait_ge(final_ready, m + 1)
                sp.dma_start(out[m], final[:, m, :]).then_inc(stored, 16)
            sp.wait_ge(stored, 16 * KT)

        @block.gpsimd
        def _(pool):
            def sums(L, k):
                f = 0 if k < ST_SWA else first(L)
                a0 = added0(L, k)
                wait_sum_read(pool, L, k)
                pool.memset(sq_sum[:, :], 0.0).then_inc(sq_added, 1)
                for j in range(STAT_TILES[k]):
                    pool.wait_ge(sq_made, made0(L, k) + j + 1)
                    pool.wait_ge(sq_added, a0 + j + 1)
                    pool.tensor_tensor(sq_sum[:, f:], sq_sum[:, f:], sq[:, f:], ALU.add).then_inc(sq_added, 1)

            def product(f, L, par, step=0):
                pool.wait_ge(silu_done, step + (L * FT + f + 1))
                pool.wait_ge(drained, step * 2 + (acc0(L) + A_F + 2 * f + 3))
                t = first(L)
                pool.tensor_tensor(up[:, par, t:], gate[:, par, t:], up[:, par, t:], ALU.mult)\
                    .then_inc(prod_ready, 1)

            sums(0, ST_ATTN)
            for L in range(DEPTH):
                for k in (ST_KV, ST_Q, ST_SWA, ST_MLA, ST_FFN):
                    sums(L, k)
                with pool.Fori(0, FT // 2) as i:
                    for c in range(2):
                        product(c, L, c, step=i * 2)
                f = first(L)
                a0, m0 = added0(L + 1, 0), made0(L + 1, 0)
                wait_sum_read(pool, L + 1, 0)
                pool.memset(sq_sum[:, :], 0.0).then_inc(sq_added, 1)
                with pool.Fori(0, KT) as i:
                    pool.wait_ge(sq_made, i + m0 + 1)
                    pool.wait_ge(sq_added, i + a0 + 1)
                    pool.tensor_tensor(sq_sum[:, f:], sq_sum[:, f:], sq[:, f:], ALU.add).then_inc(sq_added, 1)

        @block.scalar
        def _(act):
            def hi(n, width=UNIT, it=0):
                act.wait_ge(raw_landed[n % RAW], it * 16 + 16 * (n // RAW + 1))
                if n >= SPLIT:
                    wait_used(act, n - SPLIT, it)
                act.activation(w_hi[:, n % SPLIT, 0:width], raw[:, n % RAW, 0:width], ACT.Copy)\
                   .then_inc(hi_ready, 1)

            def square(src, L, k, j, f=0, step=0):
                act.wait_ge(sq_added, step + (added0(L, k) + j + 1))
                if not isinstance(step, int):
                    act.nop(nofuse=True)
                act.activation(sq[:, f:], src, ACT.Square).then_inc(sq_made, 1)

            def gained(m, gain, f):
                act.activation(u_hi[:, m, f:], h[:, m, f:], ACT.Copy, scale=gain).then_inc(uh_ready, 1)

            def root(L, k, dst, f=0):
                act.wait_ge(var_ready, stat(L, k) + 1)
                act.activation(dst[:, f:], var[:, f:], ACT.Sqrt).then_inc(r_ready, 1)

            def latent(L, j, k, jj):
                act.wait_ge(drained, acc0(L) + drain_rank(["kva", "qa0", "qa1"][j]))
                g = gn[:, L * G_LAYER + (G_KV if j == 0 else G_Q + j - 1):][:, 0:1]
                act.activation(c_hi[:, j, :], c_raw[:, j, :], ACT.Copy, scale=g).then_inc(ch_ready, 1)
                square(c_raw[:, j, :], L, k, jj)

            def swap(L, name, scale, before):
                a = PROJ.index(name)
                s = a % 4
                act.wait_ge(acc_ready, acc0(L) + a + 1)
                if before:
                    act.wait_ge(drained, acc0(L) + drain_rank(before))
                for qd in range(4):
                    o = 32 * (qd ^ 1)
                    ins = act.activation(swapped[o:o + 32, :].rearrange("p (c n) -> p c n", c=2),
                                         ps[32 * qd:32 * qd + 32, 2 * s:2 * s + 2, 0:CHUNK],
                                         ACT.Copy, scale=scale)
                ins.then_inc(swap_ready, 1)

            def attention(L):
                u0, f = L * len(BLOCKS), first(L)

                def copy_pT(i):
                    g, _, b, _, _ = BLOCKS[i]
                    U = u0 + i
                    w = len(pieces(g, b))
                    act.wait_ge(pT_done, U + 1)
                    if U >= 2:
                        act.wait_ge(pv_done, U - 1)
                    act.activation(pT[:, U % 2, 0:w * P], turned(U, 0, w), ACT.Copy).then_inc(pT_copied, 1)

                def exponential(i):
                    g, _, b, _, _ = BLOCKS[i]
                    U = u0 + i
                    n = key_range(g, b)[1] + (1 if g == 0 else 0)
                    c = U % S_RING
                    act.wait_ge(max_ready, U + 1)
                    if U >= S_RING:
                        act.wait_ge(pT_done, U - S_RING + 1)
                    act.activation(probs[:, c, 0:n], s_view(g, b, n), ACT.Exp, bias=neg_max[:, c:c + 1],
                                   accum_out=row_sum[:, c:c + 1]).then_inc(exp_ready, 1)

                for i in range(len(BLOCKS) + 4):
                    if 3 <= i < len(BLOCKS) + 3:
                        copy_pT(i - 3)
                    if i < len(BLOCKS):
                        exponential(i)
                    if i >= 13 and (i - 13) % 8 == 0:
                        pair_squares(L, (i - 13) // 8)
                    if i == ROOT_AT:
                        root(L, ST_SWA, r_kv, f)
                    if i >= MIX_AT + 1 and (i - MIX_AT - 1) % 2 == 0 and (i - MIX_AT - 1) // 2 < 4:
                        mix_part(L, (i - MIX_AT - 1) // 2)
                pair_squares(L, 7)

            def pair_squares(L, p):
                act.wait_ge(o_copied, L * 8 + p + 1)
                square(oT[:, p, first(L):], L, ST_SWA + p // 4, p % 4, first(L))

            def mix_part(L, t):
                f = first(L)
                act.wait_ge(mixf_ready, L * KT + t + 1)
                act.activation(mix_tile("hi", t)[:, f:], oT[:, t, f:], ACT.Copy).then_inc(mixh_ready, 1)

            def meta_attention(L, g):
                w = N_META + (1 if g == 0 else 0)
                act.wait_ge(m_dve, 20 * L + 10 * g + 4)
                act.activation(ms[:, :, 0:w], ms[:, :, 0:w], ACT.Exp).then_inc(m_exp, 1)

            hi(0)
            for m in range(KT):
                if m == 0:
                    act.wait_ge(consts_landed, 16)
                act.wait_ge(h_landed[m], 16)
                gained(m, gn[:, G_ATTN + m:G_ATTN + m + 1], 0)
                square(h[:, m, :], 0, ST_ATTN, m)
                if m == 3:
                    hi(1)
            for L in range(DEPTH):
                n0, f = unit0(L), first(L)
                gl = L * G_LAYER
                hi(n0 + 2)
                root(L, ST_ATTN, r_main)
                hi(n0 + 3)
                latent(L, 0, ST_KV, 0)
                hi(n0 + 4)
                latent(L, 1, ST_Q, 0)
                hi(n0 + 5)
                latent(L, 2, ST_Q, 1)
                root(L, ST_KV, r_kv)
                act.wait_ge(drained, acc0(L) + drain_rank("KRS"))
                act.activation(k_mla[64:P, :, :], kr_sum[64:P, :].unsqueeze(1).broadcast_to([64, HEADS, T]),
                               ACT.Copy).then_inc(krope_ready, 1)
                hi(n0 + 6)
                swap(L, "ka", 1.0, None)
                hi(n0 + 7)
                root(L, ST_Q, r_q)
                for j in range(4):
                    hi(n0 + 8 + j)
                    swap(L, f"q{j}", SWA_SCALE, "ka" if j == 0 else f"q{j - 1}")
                hi(n0 + 12)
                hi(n0 + 13)
                hi(n0 + 14)
                if L < DEPTH - 1:
                    for g in range(2):
                        meta_attention(L, g)
                attention(L)
                root(L, ST_MLA, r_q, f)
                for t in range(4, KT):
                    mix_part(L, t)
                for j, (m0, half) in enumerate(O_UNITS):
                    hi(n0 + U_O + j + 2)
                    if half:
                        for m in (m0, m0 + 1):
                            act.wait_ge(drained, acc0(L) + A_O + m + 1)
                            gained(m, gn[:, gl + G_FFN + m:gl + G_FFN + m + 1], f)
                            square(h[:, m, f:], L, ST_FFN, m, f)

                def silu(p, step=0):
                    act.wait_ge(drained, step * 2 + (acc0(L) + A_F + 2 * p + 2))
                    act.activation(gate[:, p % 2, f:], gate[:, p % 2, f:], ACT.Silu).then_inc(silu_done, 1)

                def act_part(p, at_tile, step=0):
                    act.wait_ge(prod_ready, step + (L * FT + p + 1))
                    if not isinstance(at_tile, int):
                        act.nop(nofuse=True)
                    act.activation(act_hi[:, at_tile, f:], up[:, p % 2, f:], ACT.Copy).then_inc(acth_ready, 1)

                for p in range(2):
                    hi(n0 + U_GU + 2 * p + 2)
                    if p == 0:
                        root(L, ST_FFN, r_main, f)
                    silu(p)
                    hi(n0 + U_GU + 2 * p + 3)
                    act_part(p, p)
                with act.Fori(0, FT // 2 - 1) as i:
                    for c in range(2):
                        hi(n0 + U_GU + 2 * c + 6, it=i)
                        silu(c + 2, step=i * 2)
                        hi(n0 + U_GU + 2 * c + 7, it=i)
                        act_part(c + 2, i * 2 + c + 2, step=i * 2)

                def down(m, step=0, at_m=None, last=False):
                    at_m = m if at_m is None else at_m
                    for c in range(4):
                        n = n0 + U_DOWN + 4 * m + 2 + c
                        if last and c >= 2:
                            if L == DEPTH - 1:
                                continue
                            hi(n)
                            continue
                        hi(n, P * DOWN_PARTS[(2 + c) % 4], it=step)
                    act.wait_ge(drained, step + (acc0(L) + A_D + m + 1))
                    if not isinstance(at_m, int):
                        act.nop(nofuse=True)
                    if L < DEPTH - 1:
                        gained(at_m, gn[:, bass.ds(at_m + (gl + G_LAYER + G_ATTN), 1)] if at_m is not m else
                               gn[:, gl + G_LAYER + G_ATTN + m:gl + G_LAYER + G_ATTN + m + 1], 0)
                    square(h[:, at_m, f:], L + 1, 0, m, f, step=step)

                with act.Fori(0, KT - 1) as i:
                    down(0, step=i, at_m=i)
                down(KT - 1, last=True)
            root(DEPTH, 0, r_main, N_META)

        @block.vector
        def _(dve):
            def lo(n, width=UNIT, it=0):
                dve.wait_ge(hi_ready, it * 4 + (n + 1))
                dve.tensor_tensor(w_lo[:, n % SPLIT, 0:width], raw[:, n % RAW, 0:width],
                                  f32(w_hi[:, n % SPLIT, 0:width]), ALU.subtract).then_inc(lo_ready, 1)

            def u_part(m, gain, f, n, step=0, at_m=None):
                at_m = m if at_m is None else at_m
                dve.wait_ge(uh_ready, step + (n + 1))
                dve.scalar_tensor_tensor(out=u_lo[:, at_m, f:], in0=h[:, at_m, f:], scalar=gain,
                                         in1=f32(u_hi[:, at_m, f:]), op0=ALU.mult, op1=ALU.subtract)\
                   .then_inc(u_ready, 1)

            def mean_square(L, k, a, slot, count, f_layer, rank=None, part=None):
                s = stat(L, k)
                v = tok_view(var[:, :], f_layer)
                if part:
                    q0 = first(f_layer) + (part - 1) * (T - first(f_layer)) // 4
                    q1 = first(f_layer) + part * (T - first(f_layer)) // 4
                    dve.wait_ge(drained, a + 1)
                    ins = dve.reciprocal(var[:, q0:q1], var[:, q0:q1])
                    if part == 4:
                        ins.then_inc(var_ready, 1)
                    return
                rank = a + 1 if rank is None else rank
                dve.wait_ge(acc_ready, a + 1)
                if s:
                    dve.wait_ge(r_ready, s)
                dve.tensor_scalar(v, acc_view(slot, f_layer), 1.0 / count, EPS, ALU.mult, ALU.add)\
                   .then_inc(drained, 1)
                if part == 0:
                    return
                dve.wait_ge(drained, rank)
                dve.reciprocal(v, v).then_inc(var_ready, 1)

            def two(ap):
                return ap.rearrange("p (c n) -> p c n", c=2)

            def proj_wait(L, name):
                a = PROJ.index(name)
                dve.wait_ge(acc_ready, acc0(L) + a + 1)
                return a % 4

            def bank(s, lo_=0, hi_=P):
                return ps[lo_:hi_, 2 * s:2 * s + 2, 0:CHUNK]

            def scaled(L, name, dst, table, lo_=0, hi_=P):
                s = proj_wait(L, name)
                return dve.tensor_tensor(two(dst), bank(s, lo_, hi_), two(table), ALU.mult)

            def rotate(L, name, dst, scale, j):
                s = proj_wait(L, name)
                dve.wait_ge(swap_ready, 5 * L + j + 1)
                if L or j:
                    dve.wait_ge(drained, acc0(L) + drain_rank(name) - 1)
                dve.scalar_tensor_tensor(out=two(rot_a[:, :]), in0=bank(s), scalar=scale,
                                         in1=two(cos_r[:, :]), op0=ALU.mult, op1=ALU.mult).then_inc(rot_step, 1)
                dve.tensor_tensor(rot_b[:, :], swapped[:, :], sin_r[:, :], ALU.mult).then_inc(rot_step, 1)
                dve.wait_ge(rot_step, 2 * (5 * L + j) + 2)
                dve.tensor_tensor(dst, rot_a[:, :], rot_b[:, :], ALU.add).then_inc(drained, 1)

            def c_part(L, j):
                g = gn[:, L * G_LAYER + (G_KV if j == 0 else G_Q + j - 1):][:, 0:1]
                dve.wait_ge(ch_ready, 3 * L + j + 1)
                dve.scalar_tensor_tensor(out=c_lo[:, j, :], in0=c_raw[:, j, :], scalar=g,
                                         in1=f32(c_hi[:, j, :]), op0=ALU.mult, op1=ALU.subtract)\
                   .then_inc(c_ready, 1)

            def values(L, name, dst, dst_meta):
                s = proj_wait(L, name)
                dve.tensor_copy(dst, ps[:, 2 * s, :].rearrange("p (b n) -> p b n", b=NB))
                dve.tensor_copy(dst_meta, ps[0:N_META, 2 * s + 1, 0:P]).then_inc(drained, 1)

            def meta_attention(L, g):
                n0 = 20 * L + 10 * g
                w = N_META + (1 if g == 0 else 0)
                mask = cst[0:N_META, C_MASK + P:C_MASK + P + N_META].unsqueeze(1)\
                    .broadcast_to([N_META, 4, N_META])
                dve.wait_ge(m_pe, 3 * (2 * L + g) + 1)
                for e in range(2):
                    s_four = ps[0:N_META, 6 + e, 0:P].rearrange("p (h n) -> p h n", h=4)[:, :, 0:N_META]
                    ins = dve.tensor_tensor(ms[:, 4 * e:4 * e + 4, 0:N_META], s_four, mask, ALU.add)
                ins.then_inc(m_dve, 1)
                sink = gn[0:N_META, L * G_LAYER + G_SINK:L * G_LAYER + G_SINK + HEADS]
                dve.tensor_copy(ms[:, :, N_META], sink).then_inc(m_dve, 1)
                dve.wait_ge(m_dve, n0 + 2)
                dve.tensor_reduce(mrow[:, 0, :], ms[:, :, 0:w], AX.X, ALU.max).then_inc(m_dve, 1)
                dve.wait_ge(m_dve, n0 + 3)
                dve.tensor_tensor(ms[:, :, 0:w], ms[:, :, 0:w],
                                  mrow[:, 0, :].unsqueeze(2).broadcast_to([N_META, HEADS, w]),
                                  ALU.subtract).then_inc(m_dve, 1)
                dve.wait_ge(m_exp, 2 * L + g + 1)
                dve.tensor_reduce(mrow[:, 1, :], ms[:, :, 0:w], AX.X, ALU.add).then_inc(m_dve, 1)
                dve.wait_ge(m_dve, n0 + 5)
                dve.reciprocal(mrow[:, 2, :], mrow[:, 1, :]).then_inc(m_dve, 1)
                dve.wait_ge(m_dve, n0 + 6)
                dve.tensor_tensor(ms[:, :, 0:N_META], ms[:, :, 0:N_META],
                                  mrow[:, 2, :].unsqueeze(2).broadcast_to([N_META, HEADS, N_META]),
                                  ALU.mult).then_inc(m_dve, 1)
                dve.wait_ge(m_pe, 3 * (2 * L + g) + 2)
                dve.tensor_copy(mpT[:, :], ps[0:N_META, 5, 0:HEADS * N_META]).then_inc(m_dve, 1)
                dve.wait_ge(m_pe, 3 * (2 * L + g) + 3)
                dve.tensor_copy(oT[:, 4 * g:4 * g + 4, 0:N_META],
                                ps[:, 6, 0:4 * N_META].rearrange("p (t n) -> p t n", t=4)).then_inc(m_dve, 2)

            def attention(L):
                u0, f = L * len(BLOCKS), first(L)

                def put_sink(i):
                    g, head, b, _, _ = BLOCKS[i]
                    n = key_range(g, b)[1]
                    col = L * G_LAYER + G_SINK + head
                    dve.wait_ge(s_ready, u0 + i + 1)
                    dve.tensor_copy(ps[:, b, n:n + 1], gn[:, col:col + 1]).then_inc(sink_put, 1)

                def row_max(i):
                    g, head, b, _, _ = BLOCKS[i]
                    U = u0 + i
                    n = key_range(g, b)[1]
                    c = U % S_RING
                    dve.wait_ge(s_ready, U + 1)
                    if g == 0:
                        n += 1
                        dve.wait_ge(sink_put, L * GB + i + 1)
                    if U >= S_RING:
                        dve.wait_ge(exp_ready, U - S_RING + 1)
                    dve.tensor_reduce(neg_max[:, c:c + 1], s_view(g, b, n), AX.X, ALU.max, negate=True)\
                       .then_inc(max_ready, 1)

                def normalise(i):
                    g, _, b, _, _ = BLOCKS[i]
                    U = u0 + i
                    c = U % S_RING
                    dve.wait_ge(exp_ready, U + 1)
                    if U >= S_RING:
                        dve.wait_ge(p_ready, U - S_RING + 1)
                    dve.reciprocal(inv_sum[:, c:c + 1], row_sum[:, c:c + 1]).then_inc(inv_ready, 1)
                    dve.wait_ge(inv_ready, U + 1)
                    cols = probs[:, c, 0:key_range(g, b)[1]]
                    dve.tensor_scalar(cols, cols, inv_sum[:, c:c + 1], None, ALU.mult).then_inc(p_ready, 1)

                def copy_o(p):
                    dve.wait_ge(pv_done, u0 + 8 * p + 8)
                    dve.tensor_copy(oT[:, p, N_META:], ps[:, O_BANK, :]).then_inc(o_copied, 1)

                put_sink(0)
                for i in range(len(BLOCKS) + 4):
                    if i >= 12 and (i - 12) % 8 == 0:
                        copy_o((i - 12) // 8)
                    if i < len(BLOCKS):
                        row_max(i)
                    if 1 <= i <= len(BLOCKS):
                        normalise(i - 1)
                    if i + 1 < GB:
                        put_sink(i + 1)
                    if i == STAT_AT:
                        mean_square(L, ST_SWA, acc0(L) + A_G, "pT", 4 * P, L, part=0)
                    if STAT_AT < i <= STAT_AT + 4:
                        mean_square(L, ST_SWA, acc0(L) + A_G, "pT", 4 * P, L, part=i - STAT_AT)
                    if i >= MIX_AT and (i - MIX_AT) % 2 == 0 and (i - MIX_AT) // 2 < 4:
                        mix_full(L, (i - MIX_AT) // 2)
                    if i >= MIX_AT + 3 and (i - MIX_AT - 3) % 2 == 0 and (i - MIX_AT - 3) // 2 < 4:
                        mix_part(dve, L, (i - MIX_AT - 3) // 2, f)
                copy_o(7)

            def mix_full(L, t):
                f, g = first(L), t // 4
                gain = gn[:, L * G_LAYER + G_SWA + t:][:, 0:1]
                if t % 4 == 0:
                    dve.wait_ge(r_ready, stat(L, ST_SWA + g) + 1)
                dve.scalar_tensor_tensor(out=oT[:, t, f:], in0=oT[:, t, f:], scalar=gain, in1=(r_kv, r_q)[g][:, f:],
                                         op0=ALU.mult, op1=ALU.mult).then_inc(mixf_ready, 1)

            lo(0)
            dve.wait_ge(consts_landed, 16)
            for m in range(KT):
                dve.wait_ge(h_landed[m], 16)
                u_part(m, gn[:, G_ATTN + m:G_ATTN + m + 1], 0, m)
                if m == 3:
                    lo(1)
            dve.wait_ge(consts_landed, 32)
            dve.tensor_copy(ident_r[:, :], ident).then_inc(masks_ready, 1)
            dve.tensor_copy(mask_r[:, :], cst[:, C_MASK:C_MASK + 2 * P]).then_inc(masks_ready, 1)
            for L in range(DEPTH):
                n0, a0, f = unit0(L), acc0(L), first(L)
                gl = L * G_LAYER
                mean_square(L, ST_ATTN, a0 + PROJ.index("S1"), 1, D_MODEL, 0, a0 + 1)
                lo(n0 + 2)
                dve.wait_ge(r_ready, stat(L, ST_ATTN) + 1)
                scaled(L, "kva", c_raw[:, 0, :], r_main[:, :]).then_inc(drained, 1)
                dve.tensor_tensor(tbl_r[64:P, :], tbl[64:P, :], r_main[64:P, :], ALU.mult).then_inc(tables_ready, 1)
                dve.tensor_tensor(cos_r[:, :], cos_t, r_main[:, :], ALU.mult).then_inc(tables_ready, 1)
                dve.tensor_tensor(sin_r[:, :], sin_t, r_main[:, :], ALU.mult).then_inc(tables_ready, 1)
                dve.wait_ge(tables_ready, 4 * L + 3)
                s = proj_wait(L, "kr")
                dve.tensor_tensor(two(kr_t[0:64, :]), bank(s, 0, 64), two(tbl_r[64:P, :]), ALU.mult)\
                   .then_inc(drained, 1)
                lo(n0 + 3)
                c_part(L, 0)
                scaled(L, "qa0", c_raw[:, 1, :], r_main[:, :]).then_inc(drained, 1)
                lo(n0 + 4)
                c_part(L, 1)
                scaled(L, "qa1", c_raw[:, 2, :], r_main[:, :]).then_inc(drained, 1)
                lo(n0 + 5)
                c_part(L, 2)
                mean_square(L, ST_KV, a0 + PROJ.index("Skv"), PROJ.index("Skv") % 4, KV_RANK, 0)
                s = proj_wait(L, "KRS")
                dve.tensor_copy(two(kr_sum[64:P, :]), bank(s, 64, P)).then_inc(drained, 1)
                lo(n0 + 6)
                dve.wait_ge(krope_ready, L + 1)
                rotate(L, "ka", k_swa[:, :], 1.0, 0)
                lo(n0 + 7)
                scaled(L, "va", vT_swa[:, :], r_main[:, :]).then_inc(drained, 1)
                mean_square(L, ST_Q, a0 + PROJ.index("Sq"), PROJ.index("Sq") % 4, Q_RANK, 0)
                for j in range(4):
                    lo(n0 + 8 + j)
                    rotate(L, f"q{j}", q_swa[:, j, :], SWA_SCALE, j + 1)
                dve.wait_ge(r_ready, stat(L, ST_Q) + 1)
                dve.scalar_tensor_tensor(out=tbl_r[:, :], in0=tbl, scalar=MLA_SCALE, in1=r_q[:, :],
                                         op0=ALU.mult, op1=ALU.mult).then_inc(tables_ready, 1)
                values(L, "VA", v_swa[:, :, :], v_swa_meta[:, :])

                def nope(j):
                    s = proj_wait(L, f"n{j}")
                    for e in range(2):
                        ins = dve.tensor_tensor(two(k_mla[0:64, 2 * j + e, :]), bank(s, 64 * e, 64 * e + 64),
                                                two(r_kv[64 * e:64 * e + 64, :]), ALU.mult)
                    ins.then_inc(drained, 1)

                for name in PROJ[PROJ.index("n0"):]:
                    if name[0] == "n":
                        nope(int(name[1]))
                    elif name[0] == "v":
                        scaled(L, name, vT_mla[:, int(name[1]), :], r_kv[:, :]).then_inc(drained, 1)
                    elif name[0] == "V":
                        j = int(name[2])
                        values(L, name, v_mla[:, :, P * j:P * j + P], v_mla_meta[:, P * j:P * j + P])
                    else:
                        j = int(name[1])
                        if j == 0:
                            dve.wait_ge(tables_ready, 4 * L + 4)
                        scaled(L, name, q_mla[:, j, :], tbl_r[:, :]).then_inc(drained, 1)
                    if name in ("v3", "H3", "H7"):
                        lo(n0 + {"v3": 12, "H3": 13, "H7": 14}[name])
                if L < DEPTH - 1:
                    for g in range(2):
                        meta_attention(L, g)
                attention(L)
                mean_square(L, ST_MLA, a0 + A_G + 1, "pT", 4 * P, L)
                for t in range(4, KT):
                    mix_full(L, t)
                    if t > 4:
                        mix_part(dve, L, t - 1, f)
                mix_part(dve, L, KT - 1, f)

                def add_h(a, slot, m, hn, step=0, at_m=None):
                    at_m = m if at_m is None else at_m
                    dve.wait_ge(acc_ready, step + (a + 1))
                    hv = tok_view(h[:, at_m, :], L)
                    dve.tensor_tensor(hv, hv, acc_view(slot, L), ALU.add).then_inc(drained, 1)

                for j, (m0, half) in enumerate(O_UNITS):
                    lo(n0 + U_O + j + 2)
                    if half:
                        for m in (m0, m0 + 1):
                            add_h(a0 + A_O + m, m % 4, m, 0)
                            if m:
                                ffn_u(dve, u_part, L, m - 1, f)
                ffn_u(dve, u_part, L, KT - 1, f)

                def scale_acc(a, slot, dst, step=0):
                    dve.wait_ge(acc_ready, step + (a + 1))
                    dve.tensor_tensor(tok_view(dst, L), acc_view(slot, L), tok_view(r_main[:, :], L), ALU.mult)\
                       .then_inc(drained, 1)

                def act_part(p, tile, step=0):
                    dve.wait_ge(acth_ready, step + (L * FT + p + 1))
                    dve.tensor_tensor(act_lo[:, tile, f:], up[:, p % 2, f:], f32(act_hi[:, tile, f:]),
                                      ALU.subtract).then_inc(act_ready, 1)

                a1 = a0 + A_F
                mean_square(L, ST_FFN, a1 + 1, 1, D_MODEL, L, a1 + 1)
                for p in range(2):
                    lo(n0 + U_GU + 2 * p + 2)
                    if p == 0:
                        dve.wait_ge(r_ready, stat(L, ST_FFN) + 1)
                    i_gate, i_up = (0, 2) if p == 0 else (3, 4)
                    scale_acc(a1 + i_gate, i_gate % 4, gate[:, p, :])
                    if p:
                        act_part(p - 1, p - 1)
                    lo(n0 + U_GU + 2 * p + 3)
                    scale_acc(a1 + i_up, i_up % 4, up[:, p, :])
                with dve.Fori(0, FT // 2 - 1) as i:
                    for c in range(2):
                        p, j = c + 2, 5 + 2 * c
                        lo(n0 + U_GU + 2 * p + 2, it=i)
                        scale_acc(a1 + j, j % 4, gate[:, c, :], step=i * 4)
                        act_part(p - 1, i * 2 + (p - 1), step=i * 2)
                        lo(n0 + U_GU + 2 * p + 3, it=i)
                        scale_acc(a1 + j + 1, (j + 1) % 4, up[:, c, :], step=i * 4)
                act_part(FT - 1, FT - 1)

                a2 = a0 + A_D
                u0 = 2 * KT * L + 2 * KT

                def down(m, step=0, it=None, last=False):
                    for c in range(4):
                        n = n0 + U_DOWN + 4 * m + 2 + c
                        if last and c >= 2:
                            if L < DEPTH - 1:
                                lo(n)
                            continue
                        lo(n, P * DOWN_PARTS[(2 + c) % 4], it=step)
                    add_h(a2 + m, m % 2, m, 0, step=step, at_m=None if it is None else it)

                def next_u(m, step=0, at_m=None):
                    if L < DEPTH - 1:
                        gbase = gl + G_LAYER + G_ATTN
                        gain = gn[:, gbase + m:gbase + m + 1] if at_m is None else \
                            gn[:, bass.ds(at_m + gbase, 1)]
                        dve.wait_ge(drained, step + (a2 + m + 1))
                        u_part(m, gain, 0, u0 + m, step=step, at_m=at_m)

                down(0)
                down(1)
                next_u(0)
                with dve.Fori(0, KT // 2 - 2) as i:
                    for c in range(2):
                        down(c + 2, step=i * 2, it=i * 2 + (c + 2))
                        next_u(c + 1, step=i * 2, at_m=i * 2 + (c + 1))
                down(KT - 2)
                next_u(KT - 3)
                down(KT - 1, last=True)
                next_u(KT - 2)
                next_u(KT - 1)
            mean_square(DEPTH, 0, acc0(DEPTH), 2, D_MODEL, DEPTH - 1)
            dve.wait_ge(r_ready, stat(DEPTH, 0) + 1)
            for m in range(KT):
                dve.scalar_tensor_tensor(out=final[:, m, :], in0=h[:, m, N_META:], scalar=gn[:, G_FINAL + m:G_FINAL + m + 1],
                                         in1=r_main[:, N_META:], op0=ALU.mult, op1=ALU.mult).then_inc(final_ready, 1)

        @block.tensor
        def _(pe):
            def split_products(outs, n, tiles, rhs, begin, end):
                for x, (j, k, m_cols) in enumerate(tiles):
                    wh = w_hi[:, n % SPLIT, j:j + m_cols]
                    wl = w_lo[:, n % SPLIT, j:j + m_cols]
                    for y, (w, r) in enumerate(((wh, rhs[0]), (wh, rhs[1]), (wl, rhs[0]))):
                        for o, (c, cn) in outs:
                            mm = pe.matmul(o, w, (r(k) if callable(r) else r[:, k, :])[:, c:c + cn], start=begin and x == 0 and y == 0,
                                           stop=end and x == len(tiles) - 1 and y == 2)
                return mm

            def acc_outs(slot, L, m_cols=P):
                if slot == "pT":
                    return [(ps[:, PT_BANK + c, 0:cn], (k, cn)) for c, (k, cn) in enumerate(chunks(L))]
                return [(ps[0:m_cols, 2 * slot + c, 0:cn], (k, cn)) for c, (k, cn) in enumerate(chunks(L))]

            def ones_product(slot, L, f):
                for o, (c, cn) in acc_outs(slot, L):
                    mm = pe.matmul(o, ones, sq_sum[:, c:c + cn], start=True, stop=True)
                return mm

            def statistics(L, k, slot, f_layer):
                pe.wait_ge(sq_added, added0(L, k) + STAT_TILES[k] + 1 if k or L < DEPTH else
                           added0(DEPTH, 0) + KT + 1)
                ones_product(slot, f_layer, 0).then_inc(acc_ready, 1)

            def project(L):
                n0, a0 = unit0(L), acc0(L)

                for a, name in enumerate(PROJ):
                    slot = a % 4
                    if a >= 4:
                        pe.wait_ge(drained, a0 + max(drain_rank(x) for x in PROJ[:a - 3]))
                    if name in UNIT_OF:
                        n = n0 + UNIT_OF[name]
                        pe.wait_ge(lo_ready, n + 1)
                        cols = 64 if name == "kr" else P
                        outs = acc_outs(slot, 0, cols)
                        for k in range(KT):
                            if name == "kva":
                                pe.wait_ge(u_ready, 2 * KT * L + k + 1)
                            mm = split_products(outs, n, [(k * P, k, cols)], (u_hi, u_lo), k == 0, k == KT - 1)
                        mm.then_inc(acc_ready, 1)
                    elif name in ("S1", "Skv", "Sq"):
                        if a == 1 and L == 0:
                            pe.wait_ge(consts_landed, 32)
                        statistics(L, {"S1": ST_ATTN, "Skv": ST_KV, "Sq": ST_Q}[name], slot, 0)
                    elif name == "KRS":
                        pe.wait_ge(drained, a0 + drain_rank("kr"))
                        for c in range(2):
                            mm = pe.matmul(ps[64:P, 2 * slot + c, 0:CHUNK], sel,
                                           kr_t[0:64, c * CHUNK:(c + 1) * CHUNK], start=True, stop=True)
                        mm.then_inc(acc_ready, 1)
                    elif name[0] == "V":
                        src = vT_swa[:, :] if name == "VA" else vT_mla[:, int(name[2]), :]
                        pe.wait_ge(drained, a0 + drain_rank("va" if name == "VA" else f"v{name[2]}"))
                        for b in range(NB):
                            pe.transpose(ps[:, 2 * slot, P * b:P * b + P],
                                         src[:, N_META + P * b:N_META + P * b + P], ident)
                        pe.transpose(ps[0:N_META, 2 * slot + 1, 0:P], src[:, 0:N_META], ident)\
                          .then_inc(acc_ready, 1)
                    elif name[0] in "nv":
                        j = int(name[1]) + (4 if name[0] == "v" else 0)
                        n = n0 + U_KV
                        if j == 0:
                            pe.wait_ge(lo_ready, n + 1)
                            pe.wait_ge(c_ready, 3 * L + 1)
                        mm = split_products(acc_outs(slot, 0), n, [(j * P, 0, P)], (c_hi, c_lo), True, True)
                        mm.then_inc(acc_ready, 1)
                    else:
                        j = int(name[1])
                        n = n0 + U_Q + j // 4
                        if j % 4 == 0:
                            pe.wait_ge(lo_ready, n + 1)
                            pe.wait_ge(c_ready, 3 * L + 3)
                        at_ = (j % 4) * 2 * P
                        mm = split_products(acc_outs(slot, 0), n, [(at_, 1, P), (at_ + P, 2, P)],
                                            (c_hi, c_lo), True, True)
                        mm.then_inc(acc_ready, 1)

            def q_rows(g, head, c0, cn):
                if g == 0:
                    r = 64 * (head // 4)
                    return q_swa[r:r + 64, head % 4, c0:c0 + cn]
                return q_mla[:, head, c0:c0 + cn]

            def k_rows(g, head, c0, cn):
                if g == 0:
                    r = 64 * (head // 4)
                    return k_swa[r:r + 64, c0:c0 + cn]
                return k_mla[:, head, c0:c0 + cn]

            def v_rows(g, head, b):
                c = 64 * (head // 4) if g == 0 else 64 * head
                if b is None:
                    return (v_swa_meta if g == 0 else v_mla_meta)[:, c:c + 64]
                return (v_swa if g == 0 else v_mla)[:, b, c:c + 64]

            def meta_attention(L, g):
                c0 = 20 * L + 10 * g
                for head in range(HEADS):
                    mm = pe.matmul(ps[0:N_META, 6 + head // 4, 32 * (head % 4):32 * (head % 4) + N_META], q_rows(g, head, 0, N_META),
                                   k_rows(g, head, 0, N_META), start=True, stop=True)
                mm.then_inc(m_pe, 1)
                pe.wait_ge(m_dve, c0 + 7)
                for head in range(HEADS):
                    mm = pe.transpose(ps[0:N_META, 5, N_META * head:N_META * head + N_META],
                                      ms[:, head, 0:N_META], cst[0:N_META, C_ID:C_ID + N_META])
                mm.then_inc(m_pe, 1)
                pe.wait_ge(m_dve, c0 + 8)
                for head in range(HEADS):
                    p, half = (head % 4, head // 4) if g == 0 else (head // 2, head % 2)
                    mm = pe.matmul(ps[64 * half:64 * half + 64, 6, N_META * p:N_META * p + N_META],
                                   v_rows(g, head, None), mpT[:, N_META * head:N_META * head + N_META],
                                   start=True, stop=True)
                mm.then_inc(m_pe, 1)
                pe.wait_ge(m_dve, c0 + 10)

            def attention(L):
                u0 = L * len(BLOCKS)

                def scores(i):
                    g, head, b, _, _ = BLOCKS[i]
                    U = u0 + i
                    k0, n, _, _ = key_range(g, b)
                    if i >= S_RING:
                        pe.wait_ge(exp_ready, U - S_RING + 1)
                        if g and b == NB - 1:
                            pe.wait_ge(pT_copied, U - S_RING + 1)
                    q = q_rows(g, head, N_META + P * b, P)
                    if g and b == NB - 1:
                        pe.matmul(ps[:, 3, S_LONG:512], q, k_rows(g, head, 0, n - P), start=True, stop=True)
                        pe.matmul(ps[:, 4, 0:P], q, k_rows(g, head, n - P, P), start=True, stop=False)
                        out_, m0 = ps[:, 4, 0:P], P
                    else:
                        pe.matmul(ps[:, b, 0:n], q, k_rows(g, head, k0, n), start=True, stop=False)
                        masked = min(n, 2 * P) if g == 0 else P
                        out_, m0 = ps[:, b, n - masked:n], 2 * P - masked
                    pe.matmul(out_, ident_r[:, :], mask_r[:, m0:2 * P], start=False, stop=True)\
                      .then_inc(s_ready, 1)

                def turn(i):
                    g, _, b, _, _ = BLOCKS[i]
                    U = u0 + i
                    pe.wait_ge(p_ready, U + 1)
                    if i >= 2:
                        pe.wait_ge(pT_copied, U - 1)
                    for x, c in enumerate(pieces(g, b)):
                        mm = pe.transpose(turned(U, x), probs[:, U % S_RING, c:c + P], ident)
                    mm.then_inc(pT_done, 1)

                def outputs(i):
                    g, head, b, p, half = BLOCKS[i]
                    U = u0 + i
                    _, _, blocks, meta = key_range(g, b)
                    pe.wait_ge(pT_copied, U + 1)
                    if i % 8 == 0 and U:
                        pe.wait_ge(o_copied, U // 8)
                    o = ps[64 * half:64 * half + 64, O_BANK, P * b:P * b + P]
                    c0 = P if meta else 0
                    if meta:
                        pe.matmul(o, v_rows(g, head, None), pT[0:N_META, U % 2, 0:P], start=True, stop=False)
                    for x, kb in enumerate(blocks):
                        mm = pe.matmul(o, v_rows(g, head, kb), pT[:, U % 2, c0 + P * x:c0 + P * x + P],
                                       start=x == 0 and not meta, stop=x == len(blocks) - 1)
                    mm.then_inc(pv_done, 1)

                scores(0)
                for i in range(len(BLOCKS) + 4):
                    if 2 <= i < len(BLOCKS) + 2:
                        turn(i - 2)
                    if i + 1 < len(BLOCKS):
                        scores(i + 1)
                    if i >= 4:
                        outputs(i - 4)
                    if i == STAT_AT:
                        pe.wait_ge(pT_copied, u0 + STAT_AT - 1)
                        statistics(L, ST_SWA, "pT", L)
                        pe.wait_ge(drained, acc0(L) + A_G + 1)

            for L in range(DEPTH):
                n0, a0 = unit0(L), acc0(L)
                project(L)
                pe.wait_ge(drained, a0 + A_G)
                pe.wait_ge(masks_ready, 2)
                pe.wait_ge(krope_ready, L + 1)
                if L < DEPTH - 1:
                    for g in range(2):
                        meta_attention(L, g)
                attention(L)

                def unit(n, slot, tiles, rhs, begin, end, step=0):
                    pe.wait_ge(lo_ready, step + (n + 1))
                    split_products(acc_outs(slot, L), n, tiles, rhs, begin, end)\
                        .then_inc(acc_ready if end else unit_used, 1)

                whole = [(k * P, k, P) for k in range(KT)]
                mix = (lambda t: mix_tile("hi", t), lambda t: mix_tile("lo", t))
                pe.wait_ge(mix_ready, L * KT + 4)
                for j, (m0, half) in enumerate(O_UNITS):
                    n = n0 + U_O + j
                    pe.wait_ge(lo_ready, n + 1)
                    for e in range(2):
                        m = m0 + e
                        if not half and m >= 4:
                            pe.wait_ge(drained, a0 + A_O + m - 3)
                        if not half and m == 3:
                            pe.wait_ge(o_copied, 8 * L + 8)
                        for k in range(4):
                            if half:
                                pe.wait_ge(mix_ready, L * KT + 4 + k + 1)
                            mm = split_products(acc_outs(m % 4, L), n, [((4 * e + k) * P, 4 * half + k, P)], mix,
                                                half == 0 and k == 0, half == 1 and k == 3)
                        if half:
                            mm.then_inc(acc_ready, 1)
                    if not half:
                        mm.then_inc(o_half_used, 1)
                    if j == 0:
                        statistics(L, ST_MLA, "pT", L)
                        pe.wait_ge(drained, a0 + A_G + 2)
                a1 = a0 + A_F
                pe.wait_ge(drained, a1)
                for j, i_acc in enumerate((0, 2, 3, 4)):
                    if j == 0:
                        pe.wait_ge(lo_ready, n0 + U_GU + 1)
                        for k in range(KT):
                            pe.wait_ge(u_ready, 2 * KT * L + KT + k + 1)
                            mm = split_products(acc_outs(0, L), n0 + U_GU, [whole[k]], (u_hi, u_lo), k == 0,
                                                k == KT - 1)
                        mm.then_inc(acc_ready, 1)
                        statistics(L, ST_FFN, 1, L)
                        continue
                    if i_acc == 4:
                        pe.wait_ge(drained, a1 + 2)
                    unit(n0 + U_GU + j, i_acc % 4, whole, (u_hi, u_lo), True, True)
                with pe.Fori(0, FT // 2 - 1) as i:
                    for c in range(4):
                        pe.wait_ge(drained, i * 4 + (a1 + 5 + c - 3))
                        unit(n0 + U_GU + 4 + c, (5 + c) % 4, whole, (u_hi, u_lo), True, True, step=i * 4)
                a2 = a0 + A_D
                pe.wait_ge(drained, a2)
                with pe.Fori(0, KT // 2) as i:
                    for c in range(2):
                        pe.wait_ge(drained, i * 2 + (a2 + c - 1))
                        for x, (k0, kn) in enumerate(zip(DOWN_AT, DOWN_PARTS)):
                            pe.wait_ge(act_ready, L * FT + k0 + kn)
                            unit(n0 + U_DOWN + 4 * c + x, c, [(k * P, k0 + k, P) for k in range(kn)],
                                 (act_hi, act_lo), x == 0, x == 3, step=i * 8)
            statistics(DEPTH, 0, 2, DEPTH - 1)


def _tables():
    pos = np.arange(T, dtype=np.float32)

    def angles(d):
        inv = np.float32(10000.0) ** (-np.arange(0, d, 2, dtype=np.float32) / np.float32(d))
        return inv.astype(np.float32)[:, None] * pos[None, :]

    a, b = angles(SWA_DIM), angles(ROPE)
    cos_a = np.concatenate([np.cos(a)] * 4)
    sin_a = np.concatenate([-np.sin(a), np.sin(a)] * 2)
    tbl = np.concatenate([np.ones((NOPE, T)), np.cos(b), np.cos(b), -np.sin(b), np.sin(b)])
    ident = np.eye(P)
    ones = np.ones((P, P))
    sel = np.zeros((P, 64))
    for j in range(64):
        sel[j % 32, j] = sel[32 + j % 32, j] = 1.0
    r, c = np.arange(P)[:, None], np.arange(P)[None, :]
    prev, cur = np.where(c > r, 0.0, NEG), np.where(c <= r, 0.0, NEG)
    return np.concatenate([ident, ones, sel, prev, cur, cos_a, sin_a, tbl], axis=1).astype(np.float32)


def _orders():
    q, k = np.arange(512), 512 + np.arange(128)
    v, qa = 640 + np.arange(128), 768 + np.arange(256)
    kva, kr = 1024 + np.arange(128), 1152 + np.arange(32)
    heads = q.reshape(HEADS, SWA_DIM)
    q_tiles = np.concatenate([np.concatenate([heads[t], heads[t + 4]]) for t in range(4)])
    swap = np.concatenate([np.arange(16, 32), np.arange(16)])
    w_in = np.concatenate([kva, kr, kr[swap], np.zeros(64, int), qa, k, v, q_tiles])
    kv = np.arange(HEADS * 128).reshape(HEADS, 128)
    w_kv = np.concatenate([kv[:, :NOPE].ravel(), kv[:, NOPE:].ravel()])
    qu = np.arange(HEADS * 96).reshape(HEADS, 96)
    w_q = np.concatenate([qu, qu[:, NOPE:][:, swap]], axis=1).ravel()
    return w_in, w_kv, w_q, q_tiles


def _tiles(w, k_tiles):
    L, K, M = w.shape
    return w.reshape(L, k_tiles, P, M // P, P).transpose(0, 3, 2, 1, 4)


def _o_units(w):
    units = [w[:, m:m + 2, :, 4 * half:4 * half + 4].transpose(0, 2, 1, 3, 4).reshape(DEPTH, P, UNIT)
             for m, half in O_UNITS]
    return np.stack(units, axis=1)


def _columns(g):
    return g.reshape(-1, P).T


def kernel(x, meta_tokens, attn_norm, w_in, q_norm, w_q_up, kv_norm, w_kv_up, sinks,
           out_norm_swa, out_norm_mla, w_o, ffn_norm, w_gate, w_up, w_down, final_norm):
    import concourse.bacc as bacc
    from concourse.bass_utils import run_bass_kernel_spmd

    o_in, o_kv, o_q, q_tiles = _orders()
    tokens = np.concatenate([np.asarray(meta_tokens), np.asarray(x)[0]], axis=0)
    w_o = np.asarray(w_o)
    w_o = np.concatenate([w_o[:, q_tiles], w_o[:, 512:]], axis=1)
    gains = []
    for l in range(DEPTH):
        gains += [_columns(np.asarray(attn_norm)[l]), _columns(np.asarray(ffn_norm)[l]),
                  _columns(np.asarray(q_norm)[l]), _columns(np.asarray(kv_norm)[l]),
                  _columns(np.asarray(out_norm_swa)[l][q_tiles]), _columns(np.asarray(out_norm_mla)[l]),
                  np.broadcast_to(np.asarray(sinks)[l][None, :], (P, HEADS))]
    gains.append(_columns(np.asarray(final_norm)))
    arrays = {
        "tokens_t": tokens.T.reshape(KT, P, T),
        "constants": _tables(),
        "gains": np.concatenate(gains, axis=1),
        "w_in_t": _tiles(np.asarray(w_in)[:, :, o_in], KT).reshape(DEPTH, 10, P, UNIT),
        "w_kv_t": np.asarray(w_kv_up)[:, :, o_kv],
        "w_q_t": _tiles(np.asarray(w_q_up)[:, :, o_q], 2).reshape(DEPTH, 2, 4, P, 2 * P)
            .transpose(0, 1, 3, 2, 4).reshape(DEPTH, 2, P, UNIT),
        "w_o_t": _o_units(_tiles(w_o, KT)),
        "w_gate_t": _tiles(np.asarray(w_gate), KT).reshape(DEPTH, FT, P, UNIT),
        "w_up_t": _tiles(np.asarray(w_up), KT).reshape(DEPTH, FT, P, UNIT),
        "w_down_t": _tiles(np.asarray(w_down), FT).reshape(DEPTH, KT, P, FT * P),
    }
    arrays = {k: np.ascontiguousarray(a) for k, a in arrays.items()}
    nc = bacc.Bacc("TRN2", target_bir_lowering=False, num_devices=1)
    args = [nc.dram_tensor(k, a.shape, mybir.dt.from_np(a.dtype), kind="ExternalInput").ap()
            for k, a in arrays.items()]
    args.append(nc.dram_tensor("out_t", (KT, P, SEQ), F32, kind="ExternalOutput").ap())
    build(nc, *args)
    r = run_bass_kernel_spmd(nc, [arrays], core_ids=[0])
    return np.ascontiguousarray(np.asarray(r.results[0]["out_t"]).reshape(D_MODEL, SEQ).T)[None]
```

```python
from contextlib import ExitStack

import numpy as np

import concourse.bass as bass
from concourse import mybir

F32 = mybir.dt.float32
F32R = mybir.dt.float32r
ALU = mybir.AluOpType
ACT = mybir.ActivationFunctionType
AX = mybir.AxisListType

P = 128
D_MODEL = 1024
DEPTH = 2
N_META = 16
SEQ = 512
T = N_META + SEQ
NB = SEQ // P
EPS = 1e-6
NEG = -1e30
HEADS = 8
SWA_DIM = 64
Q_RANK = 256
KV_RANK = 128
NOPE = 64
ROPE = 32
V_DIM = 64
SWA_SCALE = SWA_DIM ** -0.5
MLA_SCALE = (NOPE + ROPE) ** -0.5
D_FF = -(-8 * D_MODEL // (3 * 256)) * 256
KT = D_MODEL // P
FT = D_FF // P
UNIT = KT * P
CHUNK = T // 2

U_KV, U_Q, U_O, U_GU, U_DOWN = 10, 11, 13, 21, 21 + 2 * FT
DOWN_PARTS = (6, 6, 5, 5)
DOWN_AT = (0, 6, 12, 17)
UNITS = U_DOWN + KT * len(DOWN_PARTS)
RAW, SPLIT = 4, 2
O_UNITS = [(0, 0), (2, 0), (0, 1), (2, 1), (4, 0), (6, 0), (4, 1), (6, 1)]
S_RING, PT_BANK, O_BANK = 4, 5, 7
S_LONG = 512 - (T - P)
STAT_AT, MIX_AT = 42, 48
META_AT, META_BANK = (1, 14), 4

PROJ = ["kva", "S1", "kr", "qa0", "qa1", "Skv", "KRS", "ka", "Sq", "q0", "q1", "q2", "q3", "va",
        "n0", "n1", "n2", "n3", "VA", "V0", "V1", "VM", "H0", "H1", "H2", "H3", "H4", "H5", "H6", "H7"]
ACT_DRAIN = ["n0", "n1", "n2", "n3"]
DRAIN = ["S1", "kva"] + [name for name in PROJ[2:] if name not in ACT_DRAIN]
UNIT_OF = {"kva": 0, "kr": 1, "qa0": 2, "qa1": 3, "ka": 4, "q0": 5, "q1": 6, "q2": 7, "q3": 8, "va": 9}
A_G = len(PROJ)
A_O = A_G + 2
A_F = A_O + KT
A_D = A_F + 2 * FT + 1
ACCS = A_D + KT
STAT_TILES = [KT, 1, 2, 4, 4, KT]
ST_ATTN, ST_KV, ST_Q, ST_SWA, ST_MLA, ST_FFN = range(6)
STATS = len(STAT_TILES)

C_ID, C_ONES, C_SEL, C_MASK, C_COS, C_SIN, C_TBL = 0, 128, 256, 320, 576, 576 + T, 576 + 2 * T
C_END = 576 + 3 * T
G_ATTN, G_FFN, G_Q, G_KV, G_SWA, G_MLA, G_SINK, G_LAYER = 0, 8, 16, 18, 19, 23, 27, 35
G_FINAL = DEPTH * G_LAYER
G_EPS = G_FINAL + KT


def build(nc, xT, consts, gains, w_in, w_kv, w_q, w_o, w_gate, w_up, w_down, out):
    ctx = ExitStack()
    with ctx:
        base = nc.sbuf_base
        at = [-(-base // 64) * 64]

        def place(name, shape, dt=F32, offset=None):
            size = 4 * int(np.prod(shape[1:]))
            if offset is None:
                offset = at[0]
                at[0] += -(-size // 32) * 32
            return nc.alloc_sbuf_tensor_at(name, shape, dt, offset=offset)

        def sem(name):
            return ctx.enter_context(nc.semaphore(name))

        h = place("h", [P, KT, T])
        u_hi = place("u_hi", [P, KT, T], F32R)
        u_lo = place("u_lo", [P, KT, T], F32R)
        raw = place("raw", [P, RAW, UNIT])
        w_hi = place("w_hi", [P, SPLIT, UNIT], F32R)
        w_lo = place("w_lo", [P, SPLIT, UNIT], F32R)
        x0 = at[0]
        act_hi = place("act_hi", [P, FT, T], F32R)
        act_lo = place("act_lo", [P, FT, T], F32R)
        x1 = at[0]
        at[0] = x0
        q_swa = place("q_swa", [P, 4, T])
        k_swa = place("k_swa", [P, 2, T])
        v_swa = place("v_swa", [P, NB, P])
        v_swa_meta = place("v_swa_meta", [N_META, P])
        mix_at = at[0]
        q_mla = place("q_mla", [P, HEADS, T])
        k_mla = place("k_mla", [P, HEADS, T])
        mix_hi_a = place("mix_hi_a", [P, 4, T], F32R, offset=x0)
        mix_hi_b = place("mix_hi_b", [P, 4, T], F32R, offset=mix_at)
        mix_lo_b = place("mix_lo_b", [P, 4, T], F32R, offset=mix_at + 4 * KT * T)
        v_mla = place("v_mla", [P, NB, HEADS * V_DIM])
        v_mla_meta = place("v_mla_meta", [N_META, HEADS * V_DIM])
        soft_at = at[0]
        probs = place("probs", [P, S_RING, T + 1])
        pT = place("pT", [P, 2, P + NB * P])
        vT_swa = place("vT_swa", [P, T], offset=soft_at)
        o_at = at[0]
        oT = place("oT", [P, 8, T])
        c_hi = place("c_hi", [P, 3, T], F32R, offset=o_at)
        c_lo = place("c_lo", [P, 3, T], F32R, offset=o_at + 4 * 3 * T)
        sin_r = place("sin_r", [P, T], offset=o_at + 4 * 6 * T)
        cos_r = place("cos_r", [P, T], offset=o_at + 4 * 7 * T)
        r_kv = place("r_kv", [P, T])
        assert at[0] <= x1, (at[0], x1)
        at[0] = max(at[0], x1)
        cst = place("cst", [P, C_END])
        gn = place("gn", [P, G_EPS + 1])
        ident_r = place("ident_r", [P, P], F32R)
        mask_r = place("mask_r", [P, 2 * P], F32R)
        r_main = place("r_main", [P, T])
        r_q = place("r_q", [P, T])
        tbl_r = place("tbl_r", [P, T])
        rms = place("rms", [P, T])
        sq = place("sq", [P, T])
        sq_sum = place("sq_sum", [P, T])
        z = at[0]
        c_raw = place("c_raw", [P, 3, T])
        swapped = place("swapped", [P, T])
        rot_a = place("rot_a", [P, T])
        rot_b = place("rot_b", [P, T])
        mix_lo_a = place("mix_lo_a", [P, 4, T], F32R, offset=z + 2048)
        gate = place("gate", [P, 2, T], offset=z)
        up = place("up", [P, 2, T], offset=z + 8 * T)
        neg_max = place("neg_max", [P, S_RING])
        row_sum = place("row_sum", [P, S_RING])
        warm = place("warm", [P, 5 * DEPTH])
        inv_sum = place("inv_sum", [P, S_RING])
        ms = place("ms", [N_META, HEADS, N_META + 1], offset=z)
        mrow = place("mrow", [N_META, 3, HEADS], offset=z + 640)
        mpT = place("mpT", [N_META, HEADS * N_META], offset=z + 768)
        assert at[0] <= nc.sbuf_usable_end, (at[0], nc.sbuf_usable_end)
        kr_t, kr_sum = rot_a, tbl_r[0:64, :]
        first_sq = q_mla
        final = place("final", [P, KT, SEQ], offset=x0)

        ident = cst[:, C_ID:C_ID + P]
        ones = cst[:, C_ONES:C_ONES + P]
        sel = cst[0:64, C_SEL:C_SEL + 64]
        cos_t = cst[:, C_COS:C_COS + T]
        sin_t = cst[:, C_SIN:C_SIN + T]
        tbl = cst[:, C_TBL:C_TBL + T]

        ps = ctx.enter_context(nc.psum_tensor("ps", [P, 8, 512], F32))

        consts_landed = sem("consts_landed")
        h_landed = [sem(f"h_landed{k}") for k in range(KT)]
        raw_landed = [sem(f"raw_landed{k}") for k in range(RAW)]
        first_landed = sem("first_landed")
        first_hi = sem("first_hi")
        first_lo = sem("first_lo")
        hi_ready = sem("hi_ready")
        lo_ready = sem("lo_ready")
        o_half_used = sem("o_half_used")
        unit_used = sem("unit_used")
        acc_ready = sem("acc_ready")
        drained = sem("drained")
        masks_ready = sem("masks_ready")
        uh_ready = sem("uh_ready")
        u_ready = sem("u_ready")
        sq_made = sem("sq_made")
        sq_added = sem("sq_added")
        rms_ready = sem("rms_ready")
        r_ready = sem("r_ready")
        tables_ready = sem("tables_ready")
        latent_ready = sem("latent_ready")
        ch_ready = sem("ch_ready")
        c_ready = sem("c_ready")
        swap_ready = sem("swap_ready")
        rot_step = sem("rot_step")
        krope_ready = sem("krope_ready")
        n_copied = sem("n_copied")
        keys_padded = sem("keys_padded")
        s_ready = sem("s_ready")
        sink_put = sem("sink_put")
        max_ready = sem("max_ready")
        exp_ready = sem("exp_ready")
        inv_ready = sem("inv_ready")
        p_ready = sem("p_ready")
        pT_done = sem("pT_done")
        pT_copied = sem("pT_copied")
        pv_done = sem("pv_done")
        o_copied = sem("o_copied")
        m_pe = sem("m_pe")
        m_dve = sem("m_dve")
        m_exp = sem("m_exp")
        mixf_ready = sem("mixf_ready")
        mixh_ready = sem("mixh_ready")
        mix_ready = sem("mix_ready")
        silu_done = sem("silu_done")
        prod_ready = sem("prod_ready")
        acth_ready = sem("acth_ready")
        act_ready = sem("act_ready")
        final_ready = sem("final_ready")
        stored = sem("stored")

        def unit0(L):
            return L * UNITS

        def acc0(L):
            return L * ACCS

        def stat(L, k):
            return L * STATS + k

        def made0(L, k):
            return L * sum(STAT_TILES) + sum(STAT_TILES[:k])

        def added0(L, k):
            return made0(L, k) + stat(L, k)

        def stat_acc(L, k):
            names = {ST_ATTN: "S1", ST_KV: "Skv", ST_Q: "Sq"}
            if L == DEPTH:
                return acc0(DEPTH)
            return acc0(L) + (PROJ.index(names[k]) if k in names else A_G + k - ST_SWA if k < ST_FFN else A_F + 1)

        def wait_sum_read(eng, L, k):
            if stat(L, k):
                eng.wait_ge(acc_ready, (stat_acc(L, k - 1) if k else stat_acc(L - 1, STATS - 1)) + 1)

        def wait_used(eng, n, it=0):
            L, r = divmod(n, UNITS)
            if r >= U_DOWN:
                m, x = divmod(r - U_DOWN, 4)
                if x < 3:
                    eng.wait_ge(unit_used, it * 3 + (3 * (KT * L + m) + x + 1))
                else:
                    eng.wait_ge(acc_ready, it + (acc0(L) + A_D + m + 1))
                return
            if r >= U_GU:
                j = r - U_GU
                a = A_F + (j + 1 if j else 0)
            elif r >= U_O:
                m0, half = O_UNITS[r - U_O]
                if not half:
                    eng.wait_ge(o_half_used, 4 * L + sum(1 - y for _, y in O_UNITS[:r - U_O]) + 1)
                    return
                a = A_O + m0 + 1
            else:
                a = PROJ.index({U_KV: "VM", U_Q: "H3", U_Q + 1: "H7"}.get(r) or
                               next(k for k, u in UNIT_OF.items() if u == r))
            eng.wait_ge(acc_ready, it * 4 + (acc0(L) + a + 1))

        def first(L):
            return 0 if L < DEPTH - 1 else N_META

        def chunks(L):
            return [(0, CHUNK), (CHUNK, CHUNK)] if L < DEPTH - 1 else [(N_META, SEQ)]

        def acc_view(slot, L, lo=0, hi=P):
            if slot == "pT":
                return ps[lo:hi, PT_BANK:PT_BANK + 2, 0:CHUNK] if L < DEPTH - 1 else ps[lo:hi, PT_BANK, 0:SEQ]
            if L < DEPTH - 1:
                return ps[lo:hi, 2 * slot:2 * slot + 2, 0:CHUNK]
            return ps[lo:hi, 2 * slot, 0:SEQ]

        def tok_view(tile, L):
            if L < DEPTH - 1:
                return tile.rearrange("p (c n) -> p c n", c=2)
            return tile[:, N_META:T]

        def f32(ap):
            return ap.bitcast(F32)

        def drain_rank(name):
            return DRAIN.index(name) + 1

        def attn_blocks():
            for g in range(2):
                for p in range(4):
                    for half in range(2):
                        head = p + 4 * half if g == 0 else 2 * p + half
                        for b in range(NB):
                            yield g, head, b, p, half

        BLOCKS = list(attn_blocks())
        GB = len(BLOCKS) // 2

        def due(i, lag):
            return [x for x in (i - lag - 1, i - lag)
                    if 0 <= x < len(BLOCKS) and i == x + lag + (x < GB)]

        def key_range(g, b):
            diag = N_META + P * b
            if g == 0 and b:
                return diag - P, 2 * P, [b - 1, b], False
            return 0, diag + P, list(range(b + 1)), True

        def s_bank(g, b):
            return b if g == 0 else (4, 0, 1, 3)[b]

        def s_view(g, b, n):
            if g and b == NB - 1:
                return ps[:, 2:4, :].rearrange("p c n -> p (c n)")[:, S_LONG:S_LONG + n]
            return ps[:, s_bank(g, b), 0:n]

        def turned(U, x, w=1):
            g, _, b, _, _ = BLOCKS[U % len(BLOCKS)]
            if g and b == NB - 1:
                return ps[:, 4:6, :].rearrange("p c n -> p (c n)")[:, 512 - P + P * x:512 - P + P * (x + w)]
            return ps[:, PT_BANK + 1 - U % 2, P * x:P * (x + w)]

        def pieces(g, b):
            _, _, blocks, meta = key_range(g, b)
            return [0] * meta + [N_META * meta + P * x for x in range(len(blocks))]

        def mix_tile(part, t):
            if t < 4:
                return (mix_hi_a if part == "hi" else mix_lo_a)[:, t, :]
            return (mix_hi_b if part == "hi" else mix_lo_b)[:, t - 4, :]

        def mix_part(dve, L, t, f):
            dve.wait_ge(mixh_ready, L * KT + t + 1)
            dve.tensor_tensor(mix_tile("lo", t)[:, f:], oT[:, t, f:], f32(mix_tile("hi", t)[:, f:]), ALU.subtract)\
               .then_inc(mix_ready, 1)

        def ffn_u(dve, u_part, L, m, f):
            g = L * G_LAYER + G_FFN + m
            dve.wait_ge(drained, acc0(L) + A_O + m + 1)
            u_part(m, gn[:, g:g + 1], f, 2 * KT * L + KT + m)

        block = ctx.enter_context(nc.Block())

        @block.sync
        def _(sp):
            def load(n, src, width=UNIT, it=0):
                slot = n % RAW
                if n >= RAW:
                    sp.wait_ge(lo_ready, it * 4 + (n - RAW + 1))
                sp.dma_start(raw[:, slot, 0:width], src).then_inc(raw_landed[slot], 16)

            for k in range(KT):
                if k == 0:
                    sp.dma_start(gn[:, :], gains).then_inc(consts_landed, 16)
                sp.dma_start(h[:, k, :], xT[k]).then_inc(h_landed[k], 16)
                if k < 2:
                    half = slice(k * UNIT // 2, (k + 1) * UNIT // 2)
                    sp.dma_start(raw[:, 0, half], w_in[0, 0, :, half])\
                      .then_inc(first_landed if k == 0 else raw_landed[0], 16)
                if k == 4:
                    load(1, w_in[0, 1])
            sp.dma_start(cst[:, :], consts).then_inc(consts_landed, 16)
            for L in range(DEPTH):
                n0 = unit0(L)
                for j in range(2 if L == 0 else 0, 10):
                    load(n0 + j, w_in[L, j])
                load(n0 + U_KV, w_kv[L])
                for j in range(2):
                    load(n0 + U_Q + j, w_q[L, j])
                for j in range(KT):
                    load(n0 + U_O + j, w_o[L, j])
                with sp.Fori(0, FT // 2) as i:
                    for c in range(4):
                        w = w_gate if c % 2 == 0 else w_up
                        load(n0 + U_GU + c, w[L, i * 2 + c // 2], it=i)
                with sp.Fori(0, KT) as i:
                    for c, (k0, kn) in enumerate(zip(DOWN_AT, DOWN_PARTS)):
                        load(n0 + U_DOWN + c, w_down[L, i, :, k0 * P:(k0 + kn) * P], kn * P, it=i)
            for m in range(KT):
                sp.wait_ge(final_ready, m + 1)
                sp.dma_start(out[m], final[:, m, :]).then_inc(stored, 16)
            sp.wait_ge(stored, 16 * KT)

        @block.gpsimd
        def _(pool):
            def sums(L, k):
                f = 0 if k < ST_SWA else first(L)
                a0 = added0(L, k)
                wait_sum_read(pool, L, k)
                pool.memset(sq_sum[:, :], 0.0).then_inc(sq_added, 1)
                for j in range(STAT_TILES[k]):
                    pool.wait_ge(sq_made, made0(L, k) + j + 1)
                    pool.wait_ge(sq_added, a0 + j + 1)
                    src = first_sq[:, j, :] if L == 0 and k == ST_ATTN else sq[:, :]
                    pool.tensor_tensor(sq_sum[:, f:], sq_sum[:, f:], src[:, f:], ALU.add).then_inc(sq_added, 1)

            def product(f, L, par, step=0):
                pool.wait_ge(silu_done, step + (L * FT + f + 1))
                pool.wait_ge(drained, step * 2 + (acc0(L) + A_F + 2 * f + 3))
                t = first(L)
                pool.tensor_tensor(up[:, par, t:], gate[:, par, t:], up[:, par, t:], ALU.mult)\
                    .then_inc(prod_ready, 1)

            sums(0, ST_ATTN)
            for L in range(DEPTH):
                if L:
                    pool.wait_ge(acc_ready, acc0(L))
                pool.wait_ge(sq_added, added0(L, ST_KV))
                pool.memset(k_swa[64:P, 0, :], 0.0).then_inc(keys_padded, 1)
                pool.wait_ge(keys_padded, 2 * L + 1)
                pool.memset(k_swa[0:64, 1, :], 0.0).then_inc(keys_padded, 1)
                pool.wait_ge(keys_padded, 2 * L + 2)
                for k in (ST_KV, ST_Q, ST_SWA, ST_MLA, ST_FFN):
                    sums(L, k)
                with pool.Fori(0, FT // 2) as i:
                    for c in range(2):
                        product(c, L, c, step=i * 2)
                f = first(L)
                a0, m0 = added0(L + 1, 0), made0(L + 1, 0)
                wait_sum_read(pool, L + 1, 0)
                pool.memset(sq_sum[:, :], 0.0).then_inc(sq_added, 1)
                with pool.Fori(0, KT) as i:
                    pool.wait_ge(sq_made, i + m0 + 1)
                    pool.wait_ge(sq_added, i + a0 + 1)
                    pool.tensor_tensor(sq_sum[:, f:], sq_sum[:, f:], sq[:, f:], ALU.add).then_inc(sq_added, 1)

        @block.scalar
        def _(act):
            def hi(n, width=UNIT, it=0):
                act.wait_ge(raw_landed[n % RAW], it * 16 + 16 * (n // RAW + 1))
                if n >= SPLIT:
                    wait_used(act, n - SPLIT, it)
                act.activation(w_hi[:, n % SPLIT, 0:width], raw[:, n % RAW, 0:width], ACT.Copy)\
                   .then_inc(hi_ready, 1)

            def square(src, L, k, j, f=0, step=0):
                act.wait_ge(sq_added, step + (added0(L, k) + j + 1))
                if not isinstance(step, int):
                    act.nop(nofuse=True)
                act.activation(sq[:, f:], src, ACT.Square).then_inc(sq_made, 1)

            def gained(m, gain, f):
                act.activation(u_hi[:, m, f:], h[:, m, f:], ACT.Copy, scale=gain).then_inc(uh_ready, 1)

            def root(L, k, a, slot, count, f_layer):
                act.wait_ge(acc_ready, a + 1)
                if stat(L, k):
                    act.wait_ge(r_ready, stat(L, k))
                act.activation(tok_view(rms[:, :], f_layer), acc_view(slot, f_layer), ACT.Sqrt,
                               bias=gn[:, G_EPS:G_EPS + 1], scale=1.0 / count).then_inc(rms_ready, 1)

            def proj_root(L, k, name, count):
                a = PROJ.index(name)
                root(L, k, acc0(L) + a, a % 4, count, 0)

            def latent_squares(L, j, k, jj):
                act.wait_ge(drained, acc0(L) + drain_rank(["kva", "qa0", "qa1"][j]))
                square(c_raw[:, j, :], L, k, jj)

            def latent_hi(L, j):
                act.wait_ge(latent_ready, 3 * L + j + 1)
                act.activation(c_hi[:, j, :], c_raw[:, j, :], ACT.Copy).then_inc(ch_ready, 1)

            def rotary_keys(L, j):
                act.wait_ge(drained, acc0(L) + drain_rank("KRS"))
                act.activation(k_mla[64:P, 2 * j:2 * j + 2, :], kr_sum.unsqueeze(1).broadcast_to([64, 2, T]),
                               ACT.Copy).then_inc(krope_ready, 1)

            def nope(L, j):
                a = PROJ.index(f"n{j}")
                act.wait_ge(acc_ready, acc0(L) + a + 1)
                s = a % 4
                for e in range(2):
                    ins = act.activation(k_mla[0:64, 2 * j + e, :].rearrange("p (c n) -> p c n", c=2),
                                         ps[64 * e:64 * e + 64, 2 * s:2 * s + 2, 0:CHUNK], ACT.Copy)
                ins.then_inc(n_copied, 1)

            loads = iter(range(5 * DEPTH))

            def load_table(function):
                c = next(loads)
                act.activation(warm[:, c:c + 1], ones[:, 0:1], function)

            def swap(L, name, scale, before):
                a = PROJ.index(name)
                s = a % 4
                act.wait_ge(acc_ready, acc0(L) + a + 1)
                if before:
                    act.wait_ge(drained, acc0(L) + drain_rank(before))
                for qd in range(4):
                    o = 32 * (qd ^ 1)
                    ins = act.activation(swapped[o:o + 32, :].rearrange("p (c n) -> p c n", c=2),
                                         ps[32 * qd:32 * qd + 32, 2 * s:2 * s + 2, 0:CHUNK],
                                         ACT.Copy, scale=scale)
                ins.then_inc(swap_ready, 1)

            def attention(L):
                u0, f = L * len(BLOCKS), first(L)

                def copy_pT(i):
                    g, _, b, _, _ = BLOCKS[i]
                    U = u0 + i
                    w = len(pieces(g, b))
                    act.wait_ge(pT_done, U + 1)
                    if U >= 2:
                        act.wait_ge(pv_done, U - 1)
                    act.activation(pT[:, U % 2, 0:w * P], turned(U, 0, w), ACT.Copy).then_inc(pT_copied, 1)

                def exponential(i):
                    g, _, b, _, _ = BLOCKS[i]
                    U = u0 + i
                    n = key_range(g, b)[1] + (1 if g == 0 else 0)
                    c = U % S_RING
                    act.wait_ge(max_ready, U + 1)
                    if U >= S_RING:
                        act.wait_ge(pT_done, U - S_RING + 1)
                    act.activation(probs[:, c, 0:n], s_view(g, b, n), ACT.Exp, bias=neg_max[:, c:c + 1],
                                   accum_out=row_sum[:, c:c + 1]).then_inc(exp_ready, 1)

                for i in range(len(BLOCKS) + 4):
                    for x in due(i, 3):
                        copy_pT(x)
                    if i < len(BLOCKS):
                        exponential(i)
                    for g in range(2 if L < DEPTH - 1 else 0):
                        if i == META_AT[g] + 2:
                            meta_exponential(L, g)
                    for x in due(i, 6):
                        if x % 8 == 7:
                            pair_squares(L, x // 8)
                    if i == STAT_AT:
                        load_table(ACT.Sqrt)
                        root(L, ST_SWA, acc0(L) + A_G, "pT", 4 * P, L)
                        load_table(ACT.Exp)
                    if i >= MIX_AT + 1 and (i - MIX_AT - 1) % 2 == 0 and (i - MIX_AT - 1) // 2 < 4:
                        mix_part(L, (i - MIX_AT - 1) // 2)
                load_table(ACT.Sqrt)
                pair_squares(L, 7)

            def pair_squares(L, p):
                act.wait_ge(o_copied, L * 8 + p + 1)
                if p % 4 == 0 and L < DEPTH - 1:
                    act.wait_ge(m_dve, 20 * L + 10 * (p // 4 + 1))
                square(oT[:, p, first(L):], L, ST_SWA + p // 4, p % 4, first(L))

            def mix_part(L, t):
                f = first(L)
                act.wait_ge(mixf_ready, L * KT + t + 1)
                act.activation(mix_tile("hi", t)[:, f:], oT[:, t, f:], ACT.Copy).then_inc(mixh_ready, 1)

            def meta_exponential(L, g):
                w = N_META + (1 if g == 0 else 0)
                act.wait_ge(m_dve, 20 * L + 10 * g + 4)
                act.activation(ms[:, :, 0:w], ms[:, :, 0:w], ACT.Exp).then_inc(m_exp, 1)

            for m in range(KT):
                if m == 0:
                    act.wait_ge(first_landed, 16)
                    act.activation(w_hi[:, 0, 0:UNIT // 2], raw[:, 0, 0:UNIT // 2], ACT.Copy).then_inc(first_hi, 1)
                    act.wait_ge(consts_landed, 16)
                if m == 1:
                    act.wait_ge(raw_landed[0], 16)
                    act.activation(w_hi[:, 0, UNIT // 2:], raw[:, 0, UNIT // 2:], ACT.Copy).then_inc(hi_ready, 1)
                act.wait_ge(h_landed[m], 16)
                gained(m, gn[:, G_ATTN + m:G_ATTN + m + 1], 0)
                act.activation(first_sq[:, m, :], h[:, m, :], ACT.Square).then_inc(sq_made, 1)
                if m == 3:
                    hi(1)
            for L in range(DEPTH):
                n0, f = unit0(L), first(L)
                gl = L * G_LAYER
                hi(n0 + 2)
                proj_root(L, ST_ATTN, "S1", D_MODEL)
                hi(n0 + 3)
                latent_squares(L, 0, ST_KV, 0)
                hi(n0 + 4)
                latent_squares(L, 1, ST_Q, 0)
                hi(n0 + 5)
                latent_squares(L, 2, ST_Q, 1)
                proj_root(L, ST_KV, "Skv", KV_RANK)
                hi(n0 + 6)
                swap(L, "ka", 1.0, None)
                proj_root(L, ST_Q, "Sq", Q_RANK)
                for j in range(4):
                    hi(n0 + 7 + j)
                    swap(L, f"q{j}", SWA_SCALE, "ka" if j == 0 else f"q{j - 1}")
                    if j == 2:
                        for c in range(3):
                            latent_hi(L, c)
                    rotary_keys(L, j)
                hi(n0 + 11)
                for j in range(4):
                    nope(L, j)
                hi(n0 + 12)
                hi(n0 + 13)
                load_table(ACT.Exp)
                hi(n0 + 14)
                attention(L)
                hi(n0 + U_O + 2)
                root(L, ST_MLA, acc0(L) + A_G + 1, "pT", 4 * P, L)
                for t in range(4, KT):
                    mix_part(L, t)
                    if t == 5:
                        hi(n0 + U_O + 3)
                for j, (m0, half) in enumerate(O_UNITS):
                    if 2 <= j < KT - 1:
                        hi(n0 + U_O + j + 2)
                    if half:
                        for m in (m0, m0 + 1):
                            act.wait_ge(drained, acc0(L) + A_O + m + 1)
                            gained(m, gn[:, gl + G_FFN + m:gl + G_FFN + m + 1], f)
                            square(h[:, m, f:], L, ST_FFN, m, f)
                    if j == KT - 1:
                        hi(n0 + U_O + j + 2)

                def silu(p, step=0):
                    act.wait_ge(drained, step * 2 + (acc0(L) + A_F + 2 * p + 2))
                    act.activation(gate[:, p % 2, f:], gate[:, p % 2, f:], ACT.Silu).then_inc(silu_done, 1)

                def act_part(p, at_tile, step=0):
                    act.wait_ge(prod_ready, step + (L * FT + p + 1))
                    if not isinstance(at_tile, int):
                        act.nop(nofuse=True)
                    act.activation(act_hi[:, at_tile, f:], up[:, p % 2, f:], ACT.Copy).then_inc(acth_ready, 1)

                for p in range(2):
                    hi(n0 + U_GU + 2 * p + 2)
                    if p == 0:
                        root(L, ST_FFN, acc0(L) + A_F + 1, 1, D_MODEL, L)
                    silu(p)
                    hi(n0 + U_GU + 2 * p + 3)
                    act_part(p, p)
                with act.Fori(0, FT // 2 - 1) as i:
                    for c in range(2):
                        hi(n0 + U_GU + 2 * c + 6, it=i)
                        silu(c + 2, step=i * 2)
                        hi(n0 + U_GU + 2 * c + 7, it=i)
                        act_part(c + 2, i * 2 + c + 2, step=i * 2)

                load_table(ACT.Sqrt)
                def down(m, step=0, at_m=None, last=False):
                    at_m = m if at_m is None else at_m
                    for c in range(4):
                        n = n0 + U_DOWN + 4 * m + 2 + c
                        if last and c >= 2:
                            if L == DEPTH - 1:
                                continue
                            hi(n)
                            continue
                        hi(n, P * DOWN_PARTS[(2 + c) % 4], it=step)
                    act.wait_ge(drained, step + (acc0(L) + A_D + m + 1))
                    if not isinstance(at_m, int):
                        act.nop(nofuse=True)
                    if L < DEPTH - 1:
                        gained(at_m, gn[:, bass.ds(at_m + (gl + G_LAYER + G_ATTN), 1)] if at_m is not m else
                               gn[:, gl + G_LAYER + G_ATTN + m:gl + G_LAYER + G_ATTN + m + 1], 0)
                    square(h[:, at_m, f:], L + 1, 0, m, f, step=step)

                with act.Fori(0, KT - 1) as i:
                    down(0, step=i, at_m=i)
                down(KT - 1, last=True)
            root(DEPTH, 0, acc0(DEPTH), 0, D_MODEL, DEPTH - 1)

        @block.vector
        def _(dve):
            def lo(n, width=UNIT, it=0):
                dve.wait_ge(hi_ready, it * 4 + (n + 1))
                dve.tensor_tensor(w_lo[:, n % SPLIT, 0:width], raw[:, n % RAW, 0:width],
                                  f32(w_hi[:, n % SPLIT, 0:width]), ALU.subtract).then_inc(lo_ready, 1)

            def u_part(m, gain, f, n, step=0, at_m=None):
                at_m = m if at_m is None else at_m
                dve.wait_ge(uh_ready, step + (n + 1))
                dve.scalar_tensor_tensor(out=u_lo[:, at_m, f:], in0=h[:, at_m, f:], scalar=gain,
                                         in1=f32(u_hi[:, at_m, f:]), op0=ALU.mult, op1=ALU.subtract)\
                   .then_inc(u_ready, 1)

            def invert_rms(L, k, dst, f, parts=(0, 1, 2, 3)):
                dve.wait_ge(rms_ready, stat(L, k) + 1)
                for q in parts:
                    t0, t1 = f + q * (T - f) // 4, f + (q + 1) * (T - f) // 4
                    ins = dve.reciprocal(dst[:, t0:t1], rms[:, t0:t1])
                    if q in (0, 3):
                        ins.then_inc(drained if q == 0 else r_ready, 1)

            def two(ap):
                return ap.rearrange("p (c n) -> p c n", c=2)

            def proj_wait(L, name):
                a = PROJ.index(name)
                dve.wait_ge(acc_ready, acc0(L) + a + 1)
                return a % 4

            def bank(s, lo_=0, hi_=P):
                return ps[lo_:hi_, 2 * s:2 * s + 2, 0:CHUNK]

            def scaled(L, name, dst, table, lo_=0, hi_=P):
                s = proj_wait(L, name)
                return dve.tensor_tensor(two(dst), bank(s, lo_, hi_), two(table), ALU.mult)

            def rotate(L, name, dst, scale, j):
                s = proj_wait(L, name)
                dve.wait_ge(swap_ready, 5 * L + j + 1)
                if L or j:
                    dve.wait_ge(drained, acc0(L) + drain_rank(name) - 1)
                dve.scalar_tensor_tensor(out=two(rot_a[:, :]), in0=bank(s), scalar=scale,
                                         in1=two(cos_r[:, :]), op0=ALU.mult, op1=ALU.mult).then_inc(rot_step, 1)
                dve.tensor_tensor(rot_b[:, :], swapped[:, :], sin_r[:, :], ALU.mult).then_inc(rot_step, 1)
                dve.wait_ge(rot_step, 2 * (5 * L + j) + 2)
                if name == "ka":
                    dve.tensor_tensor(k_swa[0:64, 0, :], rot_a[0:64, :], rot_b[0:64, :], ALU.add)
                    dve.tensor_tensor(k_swa[64:P, 1, :], rot_a[64:P, :], rot_b[64:P, :], ALU.add)\
                       .then_inc(drained, 1)
                else:
                    dve.tensor_tensor(dst, rot_a[:, :], rot_b[:, :], ALU.add).then_inc(drained, 1)

            def latent(L, j):
                k = ST_KV if j == 0 else ST_Q
                g = gn[:, L * G_LAYER + (G_KV if j == 0 else G_Q + j - 1):][:, 0:1]
                dve.wait_ge(sq_made, made0(L, k) + max(j, 1))
                dve.wait_ge(r_ready, stat(L, k) + 1)
                dve.scalar_tensor_tensor(out=c_raw[:, j, :], in0=c_raw[:, j, :], scalar=g,
                                         in1=(r_kv if j == 0 else r_q)[:, :], op0=ALU.mult, op1=ALU.mult)\
                   .then_inc(latent_ready, 1)

            def latent_lo(L, j):
                dve.wait_ge(ch_ready, 3 * L + j + 1)
                dve.tensor_tensor(c_lo[:, j, :], c_raw[:, j, :], f32(c_hi[:, j, :]), ALU.subtract)\
                   .then_inc(c_ready, 1)

            def values(L, name, dst, dst_meta):
                s = proj_wait(L, name)
                dve.tensor_copy(dst, ps[:, 2 * s, :].rearrange("p (b n) -> p b n", b=NB))
                dve.tensor_copy(dst_meta, ps[0:N_META, 2 * s + 1, 0:P]).then_inc(drained, 1)

            def meta_masked(L, g):
                n0 = 20 * L + 10 * g
                w = N_META + (1 if g == 0 else 0)
                mask = cst[0:N_META, C_MASK + P:C_MASK + P + N_META].unsqueeze(1)\
                    .broadcast_to([N_META, HEADS, N_META])
                sink = gn[0:N_META, L * G_LAYER + G_SINK:L * G_LAYER + G_SINK + HEADS]
                dve.tensor_copy(ms[:, :, N_META], sink).then_inc(m_dve, 1)
                dve.wait_ge(m_pe, 3 * (2 * L + g) + 1)
                scores = ps[0:N_META, META_BANK, 0:256].rearrange("p (h n) -> p h n", h=HEADS)[:, :, 0:N_META]
                dve.tensor_tensor(ms[:, :, 0:N_META], scores, mask, ALU.add).then_inc(m_dve, 1)
                dve.wait_ge(m_dve, n0 + 2)
                dve.tensor_reduce(mrow[:, 0, :], ms[:, :, 0:w], AX.X, ALU.max).then_inc(m_dve, 1)
                dve.wait_ge(m_dve, n0 + 3)
                dve.tensor_tensor(ms[:, :, 0:w], ms[:, :, 0:w],
                                  mrow[:, 0, :].unsqueeze(2).broadcast_to([N_META, HEADS, w]),
                                  ALU.subtract).then_inc(m_dve, 1)

            def meta_probs(L, g):
                n0 = 20 * L + 10 * g
                w = N_META + (1 if g == 0 else 0)
                dve.wait_ge(m_exp, 2 * L + g + 1)
                dve.tensor_reduce(mrow[:, 1, :], ms[:, :, 0:w], AX.X, ALU.add).then_inc(m_dve, 1)
                dve.wait_ge(m_dve, n0 + 5)
                dve.reciprocal(mrow[:, 2, :], mrow[:, 1, :]).then_inc(m_dve, 1)
                dve.wait_ge(m_dve, n0 + 6)
                dve.tensor_tensor(ms[:, :, 0:N_META], ms[:, :, 0:N_META],
                                  mrow[:, 2, :].unsqueeze(2).broadcast_to([N_META, HEADS, N_META]),
                                  ALU.mult).then_inc(m_dve, 1)

            def meta_turned(L, g):
                dve.wait_ge(m_pe, 3 * (2 * L + g) + 2)
                dve.tensor_copy(mpT[:, :], ps[0:N_META, META_BANK, 256:256 + HEADS * N_META]).then_inc(m_dve, 1)

            def meta_out(L, g):
                dve.wait_ge(m_pe, 3 * (2 * L + g) + 3)
                dve.tensor_copy(oT[:, 4 * g:4 * g + 4, 0:N_META],
                                ps[:, META_BANK, 384:384 + 4 * N_META].rearrange("p (t n) -> p t n", t=4))\
                   .then_inc(m_dve, 2)

            def attention(L):
                u0, f = L * len(BLOCKS), first(L)

                def put_sink(i):
                    g, head, b, _, _ = BLOCKS[i]
                    n = key_range(g, b)[1]
                    col = L * G_LAYER + G_SINK + head
                    dve.wait_ge(s_ready, u0 + i + 1)
                    dve.tensor_copy(ps[:, b, n:n + 1], gn[:, col:col + 1]).then_inc(sink_put, 1)

                def row_max(i):
                    g, head, b, _, _ = BLOCKS[i]
                    U = u0 + i
                    n = key_range(g, b)[1]
                    c = U % S_RING
                    dve.wait_ge(s_ready, U + 1)
                    if g == 0:
                        n += 1
                        dve.wait_ge(sink_put, L * GB + i + 1)
                    if U >= S_RING:
                        dve.wait_ge(exp_ready, U - S_RING + 1)
                    dve.tensor_reduce(neg_max[:, c:c + 1], s_view(g, b, n), AX.X, ALU.max, negate=True)\
                       .then_inc(max_ready, 1)

                def invert(i):
                    U = u0 + i
                    c = U % S_RING
                    dve.wait_ge(exp_ready, U + 1)
                    if U >= S_RING:
                        dve.wait_ge(p_ready, U - S_RING + 1)
                    dve.reciprocal(inv_sum[:, c:c + 1], row_sum[:, c:c + 1]).then_inc(inv_ready, 1)

                def normalise(i):
                    g, _, b, _, _ = BLOCKS[i]
                    U = u0 + i
                    c = U % S_RING
                    dve.wait_ge(inv_ready, U + 1)
                    cols = probs[:, c, 0:key_range(g, b)[1]]
                    dve.tensor_scalar(cols, cols, inv_sum[:, c:c + 1], None, ALU.mult).then_inc(p_ready, 1)

                def copy_o(p):
                    dve.wait_ge(pv_done, u0 + 8 * p + 8)
                    dve.tensor_copy(oT[:, p, N_META:], ps[:, O_BANK, :]).then_inc(o_copied, 1)

                put_sink(0)
                for i in range(len(BLOCKS) + 4):
                    for x in due(i, 5):
                        if x % 8 == 7:
                            copy_o(x // 8)
                    if i <= GB:
                        for x in due(i, 1):
                            invert(x)
                        row_max(i)
                        for x in due(i, 1):
                            normalise(x)
                        if i + 1 < GB:
                            put_sink(i + 1)
                    else:
                        if i < len(BLOCKS):
                            row_max(i)
                        for x in due(i, 1):
                            invert(x)
                            normalise(x)
                    for g in range(2 if L < DEPTH - 1 else 0):
                        for step, work in ((1, meta_masked), (3, meta_probs), (5, meta_turned), (8, meta_out)):
                            if i == META_AT[g] + step:
                                work(L, g)
                    if STAT_AT < i <= STAT_AT + 4:
                        invert_rms(L, ST_SWA, r_kv, f, parts=(i - STAT_AT - 1,))
                    if i >= MIX_AT and (i - MIX_AT) % 2 == 0 and (i - MIX_AT) // 2 < 4:
                        mix_full(L, (i - MIX_AT) // 2)
                    if i >= MIX_AT + 3 and (i - MIX_AT - 3) % 2 == 0 and (i - MIX_AT - 3) // 2 < 4:
                        mix_part(dve, L, (i - MIX_AT - 3) // 2, f)
                copy_o(7)

            def mix_full(L, t):
                f, g = first(L), t // 4
                gain = gn[:, L * G_LAYER + G_SWA + t:][:, 0:1]
                if t % 4 == 0:
                    dve.wait_ge(r_ready, stat(L, ST_SWA + g) + 1)
                dve.scalar_tensor_tensor(out=oT[:, t, f:], in0=oT[:, t, f:], scalar=gain, in1=(r_kv, r_q)[g][:, f:],
                                         op0=ALU.mult, op1=ALU.mult).then_inc(mixf_ready, 1)

            dve.wait_ge(first_hi, 1)
            dve.tensor_tensor(w_lo[:, 0, 0:UNIT // 2], raw[:, 0, 0:UNIT // 2], f32(w_hi[:, 0, 0:UNIT // 2]),
                              ALU.subtract).then_inc(first_lo, 1)
            dve.wait_ge(consts_landed, 16)
            for m in range(KT):
                if m == 2:
                    dve.wait_ge(hi_ready, 1)
                    dve.tensor_tensor(w_lo[:, 0, UNIT // 2:], raw[:, 0, UNIT // 2:], f32(w_hi[:, 0, UNIT // 2:]),
                                      ALU.subtract).then_inc(lo_ready, 1)
                dve.wait_ge(h_landed[m], 16)
                u_part(m, gn[:, G_ATTN + m:G_ATTN + m + 1], 0, m)
                if m == 3:
                    lo(1)
            dve.wait_ge(consts_landed, 32)
            dve.tensor_copy(ident_r[:, :], ident).then_inc(masks_ready, 1)
            dve.tensor_copy(mask_r[:, :], cst[:, C_MASK:C_MASK + 2 * P]).then_inc(masks_ready, 1)
            for L in range(DEPTH):
                n0, a0, f = unit0(L), acc0(L), first(L)
                gl = L * G_LAYER
                invert_rms(L, ST_ATTN, r_main, 0)
                lo(n0 + 2)
                dve.wait_ge(r_ready, stat(L, ST_ATTN) + 1)
                scaled(L, "kva", c_raw[:, 0, :], r_main[:, :]).then_inc(drained, 1)
                dve.tensor_tensor(tbl_r[64:P, :], tbl[64:P, :], r_main[64:P, :], ALU.mult).then_inc(tables_ready, 1)
                dve.tensor_tensor(cos_r[:, :], cos_t, r_main[:, :], ALU.mult).then_inc(tables_ready, 1)
                dve.tensor_tensor(sin_r[:, :], sin_t, r_main[:, :], ALU.mult).then_inc(tables_ready, 1)
                dve.wait_ge(tables_ready, 3 * L + 3)
                s = proj_wait(L, "kr")
                dve.tensor_tensor(two(kr_t[0:64, :]), bank(s, 0, 64), two(tbl_r[64:P, :]), ALU.mult)\
                   .then_inc(drained, 1)
                lo(n0 + 3)
                scaled(L, "qa0", c_raw[:, 1, :], r_main[:, :]).then_inc(drained, 1)
                lo(n0 + 4)
                scaled(L, "qa1", c_raw[:, 2, :], r_main[:, :]).then_inc(drained, 1)
                lo(n0 + 5)
                invert_rms(L, ST_KV, r_kv, 0)
                s = proj_wait(L, "KRS")
                dve.tensor_copy(two(kr_sum), bank(s, 64, P)).then_inc(drained, 1)
                lo(n0 + 6)
                rotate(L, "ka", None, 1.0, 0)
                for j in range(4):
                    lo(n0 + 7 + j)
                    if j == 0:
                        invert_rms(L, ST_Q, r_q, 0, parts=(0, 1))
                    rotate(L, f"q{j}", q_swa[:, j, :], SWA_SCALE, j + 1)
                    if j == 0:
                        invert_rms(L, ST_Q, r_q, 0, parts=(2, 3))
                        latent(L, 0)
                    if j == 1:
                        latent(L, 1)
                        latent(L, 2)
                    if j == 2:
                        for c in range(3):
                            latent_lo(L, c)
                scaled(L, "va", vT_swa[:, :], r_main[:, :]).then_inc(drained, 1)
                lo(n0 + 11)
                values(L, "VA", v_swa[:, :, :], v_swa_meta[:, :])
                for j in range(2):
                    s = proj_wait(L, f"V{j}")
                    dve.tensor_copy(v_mla[:, 2 * j:2 * j + 2, :], ps[:, 2 * s:2 * s + 2, :]).then_inc(drained, 1)
                s = proj_wait(L, "VM")
                dve.tensor_copy(v_mla_meta[:, :], ps[0:N_META, 2 * s, :]).then_inc(drained, 1)
                lo(n0 + 12)
                for j in range(HEADS):
                    if j == HEADS - 1:
                        dve.wait_ge(n_copied, len(ACT_DRAIN) * (L + 1))
                    s = proj_wait(L, f"H{j}")
                    dve.scalar_tensor_tensor(out=two(q_mla[:, j, :]), in0=bank(s), scalar=MLA_SCALE, in1=two(tbl),
                                             op0=ALU.mult, op1=ALU.mult)\
                       .then_inc(drained, 1 if j < HEADS - 1 else 1 + len(ACT_DRAIN))
                    if j % 4 == 3:
                        lo(n0 + 13 + j // 4)
                attention(L)
                invert_rms(L, ST_MLA, r_q, f)
                lo(n0 + U_O + 2)
                for t in range(4, KT):
                    mix_full(L, t)
                    if t > 4:
                        mix_part(dve, L, t - 1, f)
                mix_part(dve, L, KT - 1, f)
                lo(n0 + U_O + 3)

                def add_h(a, slot, m, hn, step=0, at_m=None):
                    at_m = m if at_m is None else at_m
                    dve.wait_ge(acc_ready, step + (a + 1))
                    hv = tok_view(h[:, at_m, :], L)
                    dve.tensor_tensor(hv, hv, acc_view(slot, L), ALU.add).then_inc(drained, 1)

                for j, (m0, half) in enumerate(O_UNITS):
                    if 2 <= j < KT - 1:
                        lo(n0 + U_O + j + 2)
                    if half:
                        for m in (m0, m0 + 1):
                            add_h(a0 + A_O + m, m % 4, m, 0)
                            if m:
                                ffn_u(dve, u_part, L, m - 1, f)
                ffn_u(dve, u_part, L, KT - 1, f)
                lo(n0 + U_O + KT + 1)

                def scale_acc(a, slot, dst, step=0):
                    dve.wait_ge(acc_ready, step + (a + 1))
                    dve.tensor_tensor(tok_view(dst, L), acc_view(slot, L), tok_view(r_main[:, :], L), ALU.mult)\
                       .then_inc(drained, 1)

                def act_part(p, tile, step=0):
                    dve.wait_ge(acth_ready, step + (L * FT + p + 1))
                    dve.tensor_tensor(act_lo[:, tile, f:], up[:, p % 2, f:], f32(act_hi[:, tile, f:]),
                                      ALU.subtract).then_inc(act_ready, 1)

                a1 = a0 + A_F
                invert_rms(L, ST_FFN, r_main, f)
                for p in range(2):
                    lo(n0 + U_GU + 2 * p + 2)
                    if p == 0:
                        dve.wait_ge(r_ready, stat(L, ST_FFN) + 1)
                    i_gate, i_up = (0, 2) if p == 0 else (3, 4)
                    scale_acc(a1 + i_gate, i_gate % 4, gate[:, p, :])
                    if p:
                        act_part(p - 1, p - 1)
                    lo(n0 + U_GU + 2 * p + 3)
                    scale_acc(a1 + i_up, i_up % 4, up[:, p, :])
                with dve.Fori(0, FT // 2 - 1) as i:
                    for c in range(2):
                        p, j = c + 2, 5 + 2 * c
                        lo(n0 + U_GU + 2 * p + 2, it=i)
                        scale_acc(a1 + j, j % 4, gate[:, c, :], step=i * 4)
                        act_part(p - 1, i * 2 + (p - 1), step=i * 2)
                        lo(n0 + U_GU + 2 * p + 3, it=i)
                        scale_acc(a1 + j + 1, (j + 1) % 4, up[:, c, :], step=i * 4)
                act_part(FT - 1, FT - 1)

                a2 = a0 + A_D
                u0 = 2 * KT * L + 2 * KT

                def down(m, step=0, it=None, last=False):
                    for c in range(4):
                        n = n0 + U_DOWN + 4 * m + 2 + c
                        if last and c >= 2:
                            if L < DEPTH - 1:
                                lo(n)
                            continue
                        lo(n, P * DOWN_PARTS[(2 + c) % 4], it=step)
                    add_h(a2 + m, 1 + m % 2, m, 0, step=step, at_m=None if it is None else it)

                def next_u(m, step=0, at_m=None):
                    if L < DEPTH - 1:
                        gbase = gl + G_LAYER + G_ATTN
                        gain = gn[:, gbase + m:gbase + m + 1] if at_m is None else \
                            gn[:, bass.ds(at_m + gbase, 1)]
                        dve.wait_ge(drained, step + (a2 + m + 1))
                        u_part(m, gain, 0, u0 + m, step=step, at_m=at_m)

                down(0)
                down(1)
                next_u(0)
                with dve.Fori(0, KT // 2 - 2) as i:
                    for c in range(2):
                        down(c + 2, step=i * 2, it=i * 2 + (c + 2))
                        next_u(c + 1, step=i * 2, at_m=i * 2 + (c + 1))
                down(KT - 2)
                next_u(KT - 3)
                down(KT - 1, last=True)
                next_u(KT - 2)
                next_u(KT - 1)
            invert_rms(DEPTH, 0, r_main, N_META)
            dve.wait_ge(r_ready, stat(DEPTH, 0) + 1)
            for m in range(KT):
                dve.scalar_tensor_tensor(out=final[:, m, :], in0=h[:, m, N_META:],
                                         scalar=gn[:, G_FINAL + m:G_FINAL + m + 1],
                                         in1=r_main[:, N_META:], op0=ALU.mult, op1=ALU.mult).then_inc(final_ready, 1)

        @block.tensor
        def _(pe):
            def split_products(outs, n, tiles, rhs, begin, end):
                for x, (j, k, m_cols) in enumerate(tiles):
                    wh = w_hi[:, n % SPLIT, j:j + m_cols]
                    wl = w_lo[:, n % SPLIT, j:j + m_cols]
                    for y, (w, r) in enumerate(((wh, rhs[0]), (wh, rhs[1]), (wl, rhs[0]))):
                        for o, (c, cn) in outs:
                            tile = r(k) if callable(r) else r[:, k, :]
                            mm = pe.matmul(o, w, tile[:, c:c + cn], start=begin and x == 0 and y == 0,
                                           stop=end and x == len(tiles) - 1 and y == 2)
                return mm

            def acc_outs(slot, L, m_cols=P):
                if slot == "pT":
                    return [(ps[:, PT_BANK + c, 0:cn], (k, cn)) for c, (k, cn) in enumerate(chunks(L))]
                return [(ps[0:m_cols, 2 * slot + c, 0:cn], (k, cn)) for c, (k, cn) in enumerate(chunks(L))]

            def ones_product(slot, L, f):
                for o, (c, cn) in acc_outs(slot, L):
                    mm = pe.matmul(o, ones, sq_sum[:, c:c + cn], start=True, stop=True)
                return mm

            def statistics(L, k, slot, f_layer):
                pe.wait_ge(sq_added, added0(L, k) + STAT_TILES[k] + 1 if k or L < DEPTH else
                           added0(DEPTH, 0) + KT + 1)
                ones_product(slot, f_layer, 0).then_inc(acc_ready, 1)

            def project(L):
                n0, a0 = unit0(L), acc0(L)

                for a, name in enumerate(PROJ):
                    slot = a % 4
                    if a >= 4:
                        before = PROJ[:a - 3]
                        pe.wait_ge(drained, a0 + max(drain_rank(x) for x in before if x in DRAIN))
                        if "n0" in before:
                            pe.wait_ge(n_copied, len(ACT_DRAIN) * L + sum(x in ACT_DRAIN for x in before))
                    if name in UNIT_OF:
                        n = n0 + UNIT_OF[name]
                        pe.wait_ge(*((lo_ready, n + 1) if n else (first_lo, 1)))
                        cols = 64 if name == "kr" else P
                        outs = acc_outs(slot, 0, cols)
                        for k in range(KT):
                            if n == 0 and k == KT // 2:
                                pe.wait_ge(lo_ready, 1)
                            if name == "kva":
                                pe.wait_ge(u_ready, 2 * KT * L + k + 1)
                            mm = split_products(outs, n, [(k * P, k, cols)], (u_hi, u_lo), k == 0, k == KT - 1)
                        mm.then_inc(acc_ready, 1)
                    elif name in ("S1", "Skv", "Sq"):
                        if a == 1 and L == 0:
                            pe.wait_ge(consts_landed, 32)
                        statistics(L, {"S1": ST_ATTN, "Skv": ST_KV, "Sq": ST_Q}[name], slot, 0)
                    elif name == "KRS":
                        pe.wait_ge(drained, a0 + drain_rank("kr"))
                        for c in range(2):
                            mm = pe.matmul(ps[64:P, 2 * slot + c, 0:CHUNK], sel,
                                           kr_t[0:64, c * CHUNK:(c + 1) * CHUNK], start=True, stop=True)
                        mm.then_inc(acc_ready, 1)
                    elif name == "VA":
                        pe.wait_ge(drained, a0 + drain_rank("va"))
                        for b in range(NB):
                            pe.transpose(ps[:, 2 * slot, P * b:P * b + P],
                                         vT_swa[:, N_META + P * b:N_META + P * b + P], ident)
                        pe.transpose(ps[0:N_META, 2 * slot + 1, 0:P], vT_swa[:, 0:N_META], ident)\
                          .then_inc(acc_ready, 1)
                    elif name[0] == "V":
                        wide = slice(HEADS * NOPE, HEADS * (NOPE + V_DIM))
                        n = n0 + U_KV
                        blocks = [(0, 0, N_META)] if name == "VM" else \
                            [(c, N_META + P * (2 * int(name[1]) + c), P) for c in range(2)]
                        for c, t0, tn in blocks:
                            for y, (lat, w) in enumerate(((c_hi, w_hi), (c_hi, w_lo), (c_lo, w_hi))):
                                mm = pe.matmul(ps[0:tn, 2 * slot + c, :], lat[:, 0, t0:t0 + tn],
                                               w[:, n % SPLIT, wide], start=y == 0, stop=y == 2)
                        mm.then_inc(acc_ready, 1)
                    elif name[0] == "n":
                        j = int(name[1])
                        n = n0 + U_KV
                        if j == 0:
                            pe.wait_ge(lo_ready, n + 1)
                            pe.wait_ge(c_ready, 3 * L + 3)
                        mm = split_products(acc_outs(slot, 0), n, [(j * P, 0, P)], (c_hi, c_lo), True, True)
                        mm.then_inc(acc_ready, 1)
                    else:
                        j = int(name[1])
                        n = n0 + U_Q + j // 4
                        if j % 4 == 0:
                            pe.wait_ge(lo_ready, n + 1)
                        at_ = (j % 4) * 2 * P
                        mm = split_products(acc_outs(slot, 0), n, [(at_, 1, P), (at_ + P, 2, P)],
                                            (c_hi, c_lo), True, True)
                        mm.then_inc(acc_ready, 1)

            def q_rows(g, head, c0, cn):
                if g == 0:
                    return q_swa[:, head % 4, c0:c0 + cn]
                return q_mla[:, head, c0:c0 + cn]

            def k_rows(g, head, c0, cn):
                if g == 0:
                    return k_swa[:, head // 4, c0:c0 + cn]
                return k_mla[:, head, c0:c0 + cn]

            def v_rows(g, head, b):
                c = 64 * (head // 4) if g == 0 else 64 * head
                if b is None:
                    return (v_swa_meta if g == 0 else v_mla_meta)[:, c:c + 64]
                return (v_swa if g == 0 else v_mla)[:, b, c:c + 64]

            def meta_scores(L, g):
                if g:
                    pe.wait_ge(m_dve, 20 * L + 10)
                for head in range(HEADS):
                    mm = pe.matmul(ps[0:N_META, META_BANK, 32 * head:32 * head + N_META],
                                   q_rows(g, head, 0, N_META), k_rows(g, head, 0, N_META), start=True, stop=True)
                mm.then_inc(m_pe, 1)

            def meta_turn(L, g):
                pe.wait_ge(m_dve, 20 * L + 10 * g + 7)
                for head in range(HEADS):
                    c = 256 + N_META * head
                    mm = pe.transpose(ps[0:N_META, META_BANK, c:c + N_META], ms[:, head, 0:N_META],
                                      cst[0:N_META, C_ID:C_ID + N_META])
                mm.then_inc(m_pe, 1)

            def meta_outputs(L, g):
                pe.wait_ge(m_dve, 20 * L + 10 * g + 8)
                for head in range(HEADS):
                    p, half = (head % 4, head // 4) if g == 0 else (head // 2, head % 2)
                    c = 384 + N_META * p
                    mm = pe.matmul(ps[64 * half:64 * half + 64, META_BANK, c:c + N_META],
                                   v_rows(g, head, None), mpT[:, N_META * head:N_META * head + N_META],
                                   start=True, stop=True)
                mm.then_inc(m_pe, 1)

            def attention(L):
                u0 = L * len(BLOCKS)

                def scores(i):
                    g, head, b, _, _ = BLOCKS[i]
                    U = u0 + i
                    k0, n, _, _ = key_range(g, b)
                    if i >= S_RING:
                        pe.wait_ge(exp_ready, U - S_RING + 1)
                        if i == GB + NB - 1:
                            pe.wait_ge(exp_ready, u0 + GB)
                        if g and b == 0 and i > GB + S_RING:
                            pe.wait_ge(pT_copied, U - S_RING)
                    q = q_rows(g, head, N_META + P * b, P)
                    if i == GB and L < DEPTH - 1:
                        pe.wait_ge(m_dve, 20 * L + 20)
                    if g and b == NB - 1:
                        pe.matmul(ps[:, 2, S_LONG:512], q, k_rows(g, head, 0, n - P), start=True, stop=True)
                        pe.matmul(ps[:, 3, 0:P], q, k_rows(g, head, n - P, P), start=True, stop=False)
                        out_, m0 = ps[:, 3, 0:P], P
                    else:
                        pe.matmul(ps[:, s_bank(g, b), 0:n], q, k_rows(g, head, k0, n), start=True, stop=False)
                        masked = min(n, 2 * P) if g == 0 else P
                        out_, m0 = ps[:, s_bank(g, b), n - masked:n], 2 * P - masked
                    pe.matmul(out_, ident_r[:, :], mask_r[:, m0:2 * P], start=False, stop=True)\
                      .then_inc(s_ready, 1)

                def turn(i):
                    g, _, b, _, _ = BLOCKS[i]
                    U = u0 + i
                    pe.wait_ge(p_ready, U + 1)
                    if i >= 2:
                        pe.wait_ge(pT_copied, U - 1)
                    if g and b == NB - 1 and i < len(BLOCKS) - 1:
                        pe.wait_ge(exp_ready, U + 2)
                    for x, c in enumerate(pieces(g, b)):
                        mm = pe.transpose(turned(U, x), probs[:, U % S_RING, c:c + P], ident)
                    mm.then_inc(pT_done, 1)

                def outputs(i):
                    g, head, b, p, half = BLOCKS[i]
                    U = u0 + i
                    _, _, blocks, meta = key_range(g, b)
                    pe.wait_ge(pT_copied, U + 1)
                    if i % 8 == 0 and U:
                        pe.wait_ge(o_copied, U // 8)
                    o = ps[64 * half:64 * half + 64, O_BANK, P * b:P * b + P]
                    c0 = P if meta else 0
                    if meta:
                        pe.matmul(o, v_rows(g, head, None), pT[0:N_META, U % 2, 0:P], start=True, stop=False)
                    for x, kb in enumerate(blocks):
                        mm = pe.matmul(o, v_rows(g, head, kb), pT[:, U % 2, c0 + P * x:c0 + P * x + P],
                                       start=x == 0 and not meta, stop=x == len(blocks) - 1)
                    mm.then_inc(pv_done, 1)

                pe.wait_ge(drained, acc0(L) + drain_rank("H6"))
                scores(0)
                scores(1)
                pe.wait_ge(drained, acc0(L) + A_G)
                for i in range(len(BLOCKS) + 4):
                    for x in (i + 1, i + 2):
                        if x < len(BLOCKS) and x == i + (2 if x < GB else 1):
                            scores(x)
                    if i == STAT_AT:
                        pe.wait_ge(pT_copied, u0 + STAT_AT - 2)
                        statistics(L, ST_SWA, "pT", L)
                        pe.wait_ge(rms_ready, stat(L, ST_SWA) + 1)
                    for x in due(i, 2):
                        turn(x)
                    for x in due(i, 4):
                        outputs(x)
                    for g in range(2 if L < DEPTH - 1 else 0):
                        for step, work in ((0, meta_scores), (4, meta_turn), (7, meta_outputs)):
                            if i == META_AT[g] + step:
                                work(L, g)

            for L in range(DEPTH):
                n0, a0 = unit0(L), acc0(L)
                project(L)
                pe.wait_ge(masks_ready, 2)
                pe.wait_ge(keys_padded, 2 * L + 2)
                pe.wait_ge(krope_ready, 4 * (L + 1))
                attention(L)

                def unit(n, slot, tiles, rhs, begin, end, step=0):
                    pe.wait_ge(lo_ready, step + (n + 1))
                    split_products(acc_outs(slot, L), n, tiles, rhs, begin, end)\
                        .then_inc(acc_ready if end else unit_used, 1)

                whole = [(k * P, k, P) for k in range(KT)]
                mix = (lambda t: mix_tile("hi", t), lambda t: mix_tile("lo", t))
                pe.wait_ge(mix_ready, L * KT + 4)
                for j, (m0, half) in enumerate(O_UNITS):
                    n = n0 + U_O + j
                    pe.wait_ge(lo_ready, n + 1)
                    for k in range(4):
                        if half:
                            pe.wait_ge(mix_ready, L * KT + 4 + k + 1)
                        for m in (m0, m0 + 1):
                            if not half and k == 0 and m >= 4:
                                pe.wait_ge(drained, a0 + A_O + m - 3)
                            if not half and k == 0 and m == 3:
                                pe.wait_ge(o_copied, 8 * L + 8)
                            mm = split_products(acc_outs(m % 4, L), n,
                                                [((4 * (m - m0) + k) * P, 4 * half + k, P)], mix,
                                                half == 0 and k == 0, half == 1 and k == 3)
                            if half and k == 3:
                                mm.then_inc(acc_ready, 1)
                    if not half:
                        mm.then_inc(o_half_used, 1)
                    if j == 0:
                        statistics(L, ST_MLA, "pT", L)
                        pe.wait_ge(rms_ready, stat(L, ST_MLA) + 1)
                a1 = a0 + A_F
                for j, i_acc in enumerate((0, 2, 3, 4)):
                    if i_acc < 4:
                        pe.wait_ge(drained, a0 + A_O + 4 + i_acc + 1)
                    if j == 0:
                        pe.wait_ge(lo_ready, n0 + U_GU + 1)
                        for k in range(KT):
                            pe.wait_ge(u_ready, 2 * KT * L + KT + k + 1)
                            mm = split_products(acc_outs(0, L), n0 + U_GU, [whole[k]], (u_hi, u_lo), k == 0,
                                                k == KT - 1)
                        mm.then_inc(acc_ready, 1)
                        pe.wait_ge(drained, a0 + A_O + 4 + 2)
                        statistics(L, ST_FFN, 1, L)
                        continue
                    if i_acc == 4:
                        pe.wait_ge(drained, a1 + 2)
                    unit(n0 + U_GU + j, i_acc % 4, whole, (u_hi, u_lo), True, True)
                with pe.Fori(0, FT // 2 - 1) as i:
                    for c in range(4):
                        pe.wait_ge(drained, i * 4 + (a1 + 5 + c - 3))
                        unit(n0 + U_GU + 4 + c, (5 + c) % 4, whole, (u_hi, u_lo), True, True, step=i * 4)
                a2 = a0 + A_D
                with pe.Fori(0, KT // 2) as i:
                    for c in range(2):
                        pe.wait_ge(drained, i * 2 + (a2 + c - 1))
                        for x, (k0, kn) in enumerate(zip(DOWN_AT, DOWN_PARTS)):
                            pe.wait_ge(act_ready, L * FT + k0 + kn)
                            unit(n0 + U_DOWN + 4 * c + x, 1 + c, [(k * P, k0 + k, P) for k in range(kn)],
                                 (act_hi, act_lo), x == 0, x == 3, step=i * 8)
            statistics(DEPTH, 0, 0, DEPTH - 1)


def _tables():
    pos = np.arange(T, dtype=np.float32)

    def angles(d):
        inv = np.float32(10000.0) ** (-np.arange(0, d, 2, dtype=np.float32) / np.float32(d))
        return inv.astype(np.float32)[:, None] * pos[None, :]

    a, b = angles(SWA_DIM), angles(ROPE)
    cos_a = np.concatenate([np.cos(a)] * 4)
    sin_a = np.concatenate([-np.sin(a), np.sin(a)] * 2)
    tbl = np.concatenate([np.ones((NOPE, T)), np.cos(b), np.cos(b), -np.sin(b), np.sin(b)])
    ident = np.eye(P)
    ones = np.ones((P, P))
    sel = np.zeros((P, 64))
    for j in range(64):
        sel[j % 32, j] = sel[32 + j % 32, j] = 1.0
    r, c = np.arange(P)[:, None], np.arange(P)[None, :]
    prev, cur = np.where(c > r, 0.0, NEG), np.where(c <= r, 0.0, NEG)
    return np.concatenate([ident, ones, sel, prev, cur, cos_a, sin_a, tbl], axis=1).astype(np.float32)


def _orders():
    q, k = np.arange(512), 512 + np.arange(128)
    v, qa = 640 + np.arange(128), 768 + np.arange(256)
    kva, kr = 1024 + np.arange(128), 1152 + np.arange(32)
    heads = q.reshape(HEADS, SWA_DIM)
    q_tiles = np.concatenate([np.concatenate([heads[t], heads[t + 4]]) for t in range(4)])
    swap = np.concatenate([np.arange(16, 32), np.arange(16)])
    w_in = np.concatenate([kva, kr, kr[swap], np.zeros(64, int), qa, k, q_tiles, v])
    kv = np.arange(HEADS * 128).reshape(HEADS, 128)
    w_kv = np.concatenate([kv[:, :NOPE].ravel(), kv[:, NOPE:].ravel()])
    qu = np.arange(HEADS * 96).reshape(HEADS, 96)
    w_q = np.concatenate([qu, qu[:, NOPE:][:, swap]], axis=1).ravel()
    return w_in, w_kv, w_q, q_tiles


def _tiles(w, k_tiles):
    L, K, M = w.shape
    return w.reshape(L, k_tiles, P, M // P, P).transpose(0, 3, 2, 1, 4)


def _o_units(w):
    units = [w[:, m:m + 2, :, 4 * half:4 * half + 4].transpose(0, 2, 1, 3, 4).reshape(DEPTH, P, UNIT)
             for m, half in O_UNITS]
    return np.stack(units, axis=1)


def _columns(g):
    return g.reshape(-1, P).T


def kernel(x, meta_tokens, attn_norm, w_in, q_norm, w_q_up, kv_norm, w_kv_up, sinks,
           out_norm_swa, out_norm_mla, w_o, ffn_norm, w_gate, w_up, w_down, final_norm):
    import concourse.bacc as bacc
    from concourse.bass_utils import run_bass_kernel_spmd

    o_in, o_kv, o_q, q_tiles = _orders()
    tokens = np.concatenate([np.asarray(meta_tokens), np.asarray(x)[0]], axis=0)
    w_o = np.asarray(w_o)
    w_o = np.concatenate([w_o[:, q_tiles], w_o[:, 512:]], axis=1)
    gains = []
    for l in range(DEPTH):
        gains += [_columns(np.asarray(attn_norm)[l]), _columns(np.asarray(ffn_norm)[l]),
                  _columns(np.asarray(q_norm)[l]), _columns(np.asarray(kv_norm)[l]),
                  _columns(np.asarray(out_norm_swa)[l][q_tiles]), _columns(np.asarray(out_norm_mla)[l]),
                  np.broadcast_to(np.asarray(sinks)[l][None, :], (P, HEADS))]
    gains.append(_columns(np.asarray(final_norm)))
    gains.append(np.full((P, 1), EPS, np.float32))
    arrays = {
        "tokens_t": tokens.T.reshape(KT, P, T),
        "constants": _tables(),
        "gains": np.concatenate(gains, axis=1),
        "w_in_t": _tiles(np.asarray(w_in)[:, :, o_in], KT).reshape(DEPTH, 10, P, UNIT),
        "w_kv_t": np.asarray(w_kv_up)[:, :, o_kv],
        "w_q_t": _tiles(np.asarray(w_q_up)[:, :, o_q], 2).reshape(DEPTH, 2, 4, P, 2 * P)
            .transpose(0, 1, 3, 2, 4).reshape(DEPTH, 2, P, UNIT),
        "w_o_t": _o_units(_tiles(w_o, KT)),
        "w_gate_t": _tiles(np.asarray(w_gate), KT).reshape(DEPTH, FT, P, UNIT),
        "w_up_t": _tiles(np.asarray(w_up), KT).reshape(DEPTH, FT, P, UNIT),
        "w_down_t": _tiles(np.asarray(w_down), FT).reshape(DEPTH, KT, P, FT * P),
    }
    arrays = {k: np.ascontiguousarray(a) for k, a in arrays.items()}
    nc = bacc.Bacc("TRN2", target_bir_lowering=False, num_devices=1)
    args = [nc.dram_tensor(k, a.shape, mybir.dt.from_np(a.dtype), kind="ExternalInput").ap()
            for k, a in arrays.items()]
    args.append(nc.dram_tensor("out_t", (KT, P, SEQ), F32, kind="ExternalOutput").ap())
    build(nc, *args)
    r = run_bass_kernel_spmd(nc, [arrays], core_ids=[0])
    return np.ascontiguousarray(np.asarray(r.results[0]["out_t"]).reshape(D_MODEL, SEQ).T)[None]
```
